# Optimizing a Trainium2 kernel written in Bass

```python
import math
import jax, jax.numpy as jnp
from jax import lax
import numpy as np

D_MODEL = 1024
BATCH = 1
SEQ = 256
DEPTH = 2

N_MIXERS = 2
N_A = (DEPTH + 1) // 2
N_B = DEPTH // 2

SSM_EXPAND = 2
D_INNER = SSM_EXPAND * D_MODEL
SSM_HEAD_DIM = 64
SSM_HEADS = D_INNER // SSM_HEAD_DIM
SSM_GROUPS = 8
SSM_HPG = SSM_HEADS // SSM_GROUPS
SSM_STATE = 128
CONV_K = 4
CONV_DIM = D_INNER + 2 * SSM_GROUPS * SSM_STATE
SSM_IN_DIM = D_INNER + CONV_DIM + SSM_HEADS
NORM_GROUP = D_INNER // SSM_GROUPS
CHUNK = 128
DT_MIN = 0.001
DT_MAX = 0.1

MLA_HEADS = 16
Q_LORA = 384
KV_LORA = 256
QK_NOPE = 64
QK_ROPE = 32
V_DIM = 64
QK_DIM = QK_NOPE + QK_ROPE
MLA_IN_DIM = Q_LORA + KV_LORA + QK_ROPE
ROPE_THETA = 10000.0
Q_BLOCK = 128

D_FF = 2816
EPS = 1e-6


def rms_norm(x, w):
    xf = x.astype(jnp.float32)
    y = xf * lax.rsqrt(jnp.mean(xf * xf, axis=-1, keepdims=True) + EPS)
    return (y * w.astype(jnp.float32)).astype(x.dtype)

def swiglu(h, w_gate, w_up, w_down):
    return (jax.nn.silu(h @ w_gate) * (h @ w_up)) @ w_down

def causal_depthwise_conv(u, w, b):
    y = lax.conv_general_dilated(u, w[:, None, :].astype(u.dtype), window_strides=(1,),
                                 padding=[(CONV_K - 1, 0)],
                                 dimension_numbers=("NWC", "WIO", "NWC"),
                                 feature_group_count=u.shape[-1])
    return y + b

def ssd_chunked(xs, dt, a, bm, cm):
    b, s = xs.shape[:2]
    nc = s // CHUNK

    def to_chunks(t):
        return jnp.swapaxes(t.reshape((b, nc, CHUNK) + t.shape[2:]), 0, 1)

    mask = jnp.tril(jnp.ones((CHUNK, CHUNK), dtype=bool))[None, :, :, None, None]

    def step(state, inp):
        xc, dtc, bc, cc = inp
        acs = jnp.cumsum(dtc * a, axis=1)
        seg = acs[:, :, None] - acs[:, None, :]
        decay = jnp.exp(jnp.where(mask, seg, -jnp.inf))
        cb = jnp.einsum("blgn,bsgn->blsg", cc, bc)
        xdt = xc * dtc[..., None]
        y_diag = jnp.einsum("blsg,blsgr,bsgrp->blgrp", cb, decay, xdt)
        y_off = jnp.einsum("blgn,bgrpn->blgrp", cc, state) * jnp.exp(acs)[..., None]
        decay_to_end = jnp.exp(acs[:, -1:] - acs)
        new_state = (state * jnp.exp(acs[:, -1])[..., None, None]
                     + jnp.einsum("bsgn,bsgr,bsgrp->bgrpn", bc, decay_to_end, xdt))
        return new_state, y_diag + y_off

    state0 = jnp.zeros((b, SSM_GROUPS, SSM_HPG, SSM_HEAD_DIM, SSM_STATE), jnp.float32)
    _, ys = lax.scan(step, state0, (to_chunks(xs), to_chunks(dt), to_chunks(bm), to_chunks(cm)))
    return jnp.swapaxes(ys, 0, 1).reshape(xs.shape)

def mamba2_mixer(h, w_in, conv_w, conv_b, dt_bias, a_log, d_skip, norm_w, w_out):
    b, s, _ = h.shape
    proj = h @ w_in
    z = proj[..., :D_INNER]
    xbc = proj[..., D_INNER:D_INNER + CONV_DIM]
    dt = proj[..., D_INNER + CONV_DIM:]
    xbc = jax.nn.silu(causal_depthwise_conv(xbc, conv_w, conv_b))
    xs = xbc[..., :D_INNER].astype(jnp.float32).reshape(b, s, SSM_GROUPS, SSM_HPG, SSM_HEAD_DIM)
    bm = xbc[..., D_INNER:D_INNER + SSM_GROUPS * SSM_STATE].astype(jnp.float32).reshape(b, s, SSM_GROUPS, SSM_STATE)
    cm = xbc[..., D_INNER + SSM_GROUPS * SSM_STATE:].astype(jnp.float32).reshape(b, s, SSM_GROUPS, SSM_STATE)
    dt = jax.nn.softplus(dt.astype(jnp.float32) + dt_bias.astype(jnp.float32)).reshape(b, s, SSM_GROUPS, SSM_HPG)
    a = (-jnp.exp(a_log.astype(jnp.float32))).reshape(SSM_GROUPS, SSM_HPG)
    y = ssd_chunked(xs, dt, a, bm, cm)
    y = y + d_skip.astype(jnp.float32).reshape(SSM_GROUPS, SSM_HPG)[:, :, None] * xs
    g = (y.reshape(b, s, D_INNER) * jax.nn.silu(z.astype(jnp.float32))).reshape(b, s, SSM_GROUPS, NORM_GROUP)
    g = g * lax.rsqrt(jnp.mean(g * g, axis=-1, keepdims=True) + EPS)
    g = g.reshape(b, s, D_INNER) * norm_w.astype(jnp.float32)
    return g.astype(h.dtype) @ w_out

def rope_cos_sin(positions):
    inv_freq = 1.0 / (ROPE_THETA ** (jnp.arange(0, QK_ROPE, 2, dtype=jnp.float32) / QK_ROPE))
    ang = positions.astype(jnp.float32)[..., None] * inv_freq
    return jnp.cos(ang), jnp.sin(ang)

def apply_rope(x, cos, sin):
    xf = x.astype(jnp.float32)
    x1, x2 = xf[..., :QK_ROPE // 2], xf[..., QK_ROPE // 2:]
    return jnp.concatenate([x1 * cos - x2 * sin, x2 * cos + x1 * sin], axis=-1).astype(x.dtype)

def causal_block_attention(q_nope, q_rope, k_nope, k_rope, v):
    s = q_nope.shape[1]
    scale = QK_DIM ** -0.5
    outs = []
    for i in range(s // Q_BLOCK):
        q0 = i * Q_BLOCK
        kend = q0 + Q_BLOCK
        sc = (jnp.einsum("bqhd,bkhd->bhqk", q_nope[:, q0:kend], k_nope[:, :kend])
              + jnp.einsum("bqhr,bkr->bhqk", q_rope[:, q0:kend], k_rope[:, :kend]))
        sc = sc.astype(jnp.float32) * scale
        qi = q0 + jnp.arange(Q_BLOCK)
        ki = jnp.arange(kend)
        sc = jnp.where(ki[None, :] <= qi[:, None], sc, -jnp.inf)
        p = jax.nn.softmax(sc, axis=-1).astype(v.dtype)
        outs.append(jnp.einsum("bhqk,bkhd->bqhd", p, v[:, :kend]))
    return jnp.concatenate(outs, axis=1)

def mla_mixer(h, positions, w_in, q_a_norm, kv_a_norm, w_q_b, w_kv_b, q_norm, k_norm, w_out):
    b, s, _ = h.shape
    proj = h @ w_in
    cq = rms_norm(proj[..., :Q_LORA], q_a_norm)
    ckv = rms_norm(proj[..., Q_LORA:Q_LORA + KV_LORA], kv_a_norm)
    k_rope = proj[..., Q_LORA + KV_LORA:]
    q = (cq @ w_q_b).reshape(b, s, MLA_HEADS, QK_DIM)
    kv = (ckv @ w_kv_b).reshape(b, s, MLA_HEADS, QK_NOPE + V_DIM)
    q_nope, q_rope = q[..., :QK_NOPE], q[..., QK_NOPE:]
    k_nope, v = kv[..., :QK_NOPE], kv[..., QK_NOPE:]
    q_nope = rms_norm(q_nope, q_norm[:QK_NOPE])
    q_rope = rms_norm(q_rope, q_norm[QK_NOPE:])
    k_nope = rms_norm(k_nope, k_norm[:QK_NOPE])
    k_rope = rms_norm(k_rope, k_norm[QK_NOPE:])
    cos, sin = rope_cos_sin(positions)
    q_rope = apply_rope(q_rope, cos[:, :, None], sin[:, :, None])
    k_rope = apply_rope(k_rope, cos, sin)
    o = causal_block_attention(q_nope, q_rope, k_nope, k_rope, v)
    return o.reshape(b, s, MLA_HEADS * V_DIM) @ w_out

def first_inputs(seed: int = 0) -> dict:
    key = jax.random.key(seed)
    ks = jax.random.split(key, 24)
    f32 = jnp.float32

    def nrm(k, shape, fan_in):
        return jax.random.normal(k, shape, f32) * fan_in ** -0.5

    def gain(k, shape):
        return 1.0 + 0.05 * jax.random.normal(k, shape, f32)

    x = jax.random.normal(ks[0], (BATCH, SEQ, D_MODEL), f32)
    offs = jax.random.randint(ks[1], (BATCH, 1), 0, 512, dtype=jnp.int32)
    positions = (jnp.arange(SEQ, dtype=jnp.int32)[None, :] + offs).astype(jnp.int32)

    norm_w = gain(ks[2], (DEPTH, 3, D_MODEL))
    ffn_w_gate = nrm(ks[3], (DEPTH, 2, D_MODEL, D_FF), D_MODEL)
    ffn_w_up = nrm(ks[4], (DEPTH, 2, D_MODEL, D_FF), D_MODEL)
    ffn_w_down = nrm(ks[5], (DEPTH, 2, D_FF, D_MODEL), D_FF)

    ssm_w_in = nrm(ks[6], (N_A, D_MODEL, SSM_IN_DIM), D_MODEL)
    ssm_conv_w = nrm(ks[7], (N_A, CONV_K, CONV_DIM), CONV_K)
    ssm_conv_b = 0.02 * jax.random.normal(ks[8], (N_A, CONV_DIM), f32)
    u = jax.random.uniform(ks[9], (N_A, SSM_HEADS), f32)
    dt0 = jnp.exp(u * (math.log(DT_MAX) - math.log(DT_MIN)) + math.log(DT_MIN))
    ssm_dt_bias = dt0 + jnp.log(-jnp.expm1(-dt0))
    ssm_a_log = jnp.log(jax.random.uniform(ks[10], (N_A, SSM_HEADS), f32, minval=1.0, maxval=16.0))
    ssm_d = 1.0 + 0.1 * jax.random.normal(ks[11], (N_A, SSM_HEADS), f32)
    ssm_norm_w = gain(ks[12], (N_A, D_INNER))
    ssm_w_out = nrm(ks[13], (N_A, D_INNER, D_MODEL), D_INNER)

    mla_w_in = nrm(ks[14], (N_B, D_MODEL, MLA_IN_DIM), D_MODEL)
    mla_q_a_norm = gain(ks[15], (N_B, Q_LORA))
    mla_kv_a_norm = gain(ks[16], (N_B, KV_LORA))
    mla_w_q_b = nrm(ks[17], (N_B, Q_LORA, MLA_HEADS * QK_DIM), Q_LORA)
    mla_w_kv_b = nrm(ks[18], (N_B, KV_LORA, MLA_HEADS * (QK_NOPE + V_DIM)), KV_LORA)
    mla_q_norm = gain(ks[19], (N_B, QK_DIM))
    mla_k_norm = gain(ks[20], (N_B, QK_DIM))
    mla_w_out = nrm(ks[21], (N_B, MLA_HEADS * V_DIM, D_MODEL), MLA_HEADS * V_DIM)

    return {"x": x, "positions": positions, "norm_w": norm_w,
            "ffn_w_gate": ffn_w_gate, "ffn_w_up": ffn_w_up, "ffn_w_down": ffn_w_down,
            "ssm_w_in": ssm_w_in, "ssm_conv_w": ssm_conv_w, "ssm_conv_b": ssm_conv_b,
            "ssm_dt_bias": ssm_dt_bias, "ssm_a_log": ssm_a_log, "ssm_d": ssm_d,
            "ssm_norm_w": ssm_norm_w, "ssm_w_out": ssm_w_out,
            "mla_w_in": mla_w_in, "mla_q_a_norm": mla_q_a_norm, "mla_kv_a_norm": mla_kv_a_norm,
            "mla_w_q_b": mla_w_q_b, "mla_w_kv_b": mla_w_kv_b, "mla_q_norm": mla_q_norm,
            "mla_k_norm": mla_k_norm, "mla_w_out": mla_w_out}

def first_block(x, positions, norm_w, ffn_w_gate, ffn_w_up, ffn_w_down,
              ssm_w_in, ssm_conv_w, ssm_conv_b, ssm_dt_bias, ssm_a_log, ssm_d,
              ssm_norm_w, ssm_w_out,
              mla_w_in, mla_q_a_norm, mla_kv_a_norm, mla_w_q_b, mla_w_kv_b,
              mla_q_norm, mla_k_norm, mla_w_out):
    for i in range(DEPTH):
        x = x + 0.5 * swiglu(rms_norm(x, norm_w[i, 0]), ffn_w_gate[i, 0], ffn_w_up[i, 0], ffn_w_down[i, 0])
        h = rms_norm(x, norm_w[i, 1])
        j = i // N_MIXERS
        if i % N_MIXERS == 0:
            x = x + mamba2_mixer(h, ssm_w_in[j], ssm_conv_w[j], ssm_conv_b[j], ssm_dt_bias[j],
                                 ssm_a_log[j], ssm_d[j], ssm_norm_w[j], ssm_w_out[j])
        else:
            x = x + mla_mixer(h, positions, mla_w_in[j], mla_q_a_norm[j], mla_kv_a_norm[j],
                              mla_w_q_b[j], mla_w_kv_b[j], mla_q_norm[j], mla_k_norm[j], mla_w_out[j])
        x = x + 0.5 * swiglu(rms_norm(x, norm_w[i, 2]), ffn_w_gate[i, 1], ffn_w_up[i, 1], ffn_w_down[i, 1])
    return x


N_A_LAYERS = DEPTH // 2
N_B_LAYERS = DEPTH - N_A_LAYERS
CONV_WIDTH = 3
N_HEADS = 8
HEAD_DIM = 64
ATT_WIDTH = N_HEADS * HEAD_DIM
RMS_EPS = 1e-6


def _rmsnorm(x, g):
    xf = x.astype(jnp.float32)
    y = xf * lax.rsqrt(jnp.mean(xf * xf, axis=-1, keepdims=True) + RMS_EPS)
    return (y * g.astype(jnp.float32)).astype(x.dtype)

def _causal_depthwise_conv(u, w):
    return lax.conv_general_dilated(
        u, w[:, None, :].astype(u.dtype),
        window_strides=(1,),
        padding=[(CONV_WIDTH - 1, 0)],
        dimension_numbers=("NWC", "WIO", "NWC"),
        feature_group_count=u.shape[-1])

def _short_conv_mixer(h, w_in, w_conv, w_out):
    u = h @ w_in
    b_gate, c_gate, xin, g = jnp.split(u, 4, axis=-1)
    y = b_gate * _causal_depthwise_conv(c_gate * xin, w_conv)
    return (y * jax.nn.silu(g)) @ w_out

def _stick_breaking_attention(q, k, v):
    seq = q.shape[2]
    n_blocks = seq // Q_BLOCK
    scale = HEAD_DIM ** -0.5
    qf = q.astype(jnp.float32)
    kf = k.astype(jnp.float32)
    vf = v.astype(jnp.float32)
    outs = []
    for blk in range(n_blocks):
        q0 = blk * Q_BLOCK
        kl = q0 + Q_BLOCK
        qb = qf[:, :, q0:kl]
        z = jnp.einsum("bhqd,bhkd->bhqk", qb, kf[:, :, :kl]) * scale
        q_pos = q0 + jnp.arange(Q_BLOCK)
        mask = jnp.arange(kl)[None, :] < q_pos[:, None]
        log_one_minus = jnp.where(mask, jax.nn.log_sigmoid(-z), 0.0)
        rev = lax.cumsum(log_one_minus, axis=3, reverse=True)
        weights = jnp.exp(jnp.where(mask, z + rev, -jnp.inf))
        outs.append(jnp.einsum("bhqk,bhkd->bhqd", weights, vf[:, :, :kl]))
    o = jnp.concatenate(outs, axis=2)
    return o.astype(q.dtype)

def second_inputs(seed: int = 0) -> dict:
    key = jax.random.key(seed)
    ks = jax.random.split(key, 12)
    D = D_MODEL
    s = D ** -0.5
    f32 = jnp.float32
    return {
        "x": jax.random.normal(ks[0], (BATCH, SEQ, D), f32),
        "norm_a": 1.0 + 0.02 * jax.random.normal(ks[1], (N_A_LAYERS, D), f32),
        "w_in_a": s * jax.random.normal(ks[2], (N_A_LAYERS, D, 4 * D), f32),
        "conv_a": (CONV_WIDTH ** -0.5) * jax.random.normal(ks[3], (N_A_LAYERS, CONV_WIDTH, D), f32),
        "w_out_a": s * jax.random.normal(ks[4], (N_A_LAYERS, D, D), f32),
        "norm_kv": 1.0 + 0.02 * jax.random.normal(ks[5], (D,), f32),
        "w_kv": s * jax.random.normal(ks[6], (D, 2 * ATT_WIDTH), f32),
        "norm_b": 1.0 + 0.02 * jax.random.normal(ks[7], (N_B_LAYERS, D), f32),
        "w_in_b": s * jax.random.normal(ks[8], (N_B_LAYERS, D, 2 * ATT_WIDTH), f32),
        "w_out_b": (ATT_WIDTH ** -0.5) * jax.random.normal(ks[9], (N_B_LAYERS, ATT_WIDTH, D), f32),
        "norm_f": 1.0 + 0.02 * jax.random.normal(ks[10], (D,), f32),
    }

def second_block(x, norm_a, w_in_a, conv_a, w_out_a, norm_kv, w_kv, norm_b, w_in_b, w_out_b, norm_f):
    bsz, seq, _ = x.shape
    k = v = None
    for layer in range(DEPTH):
        if layer < N_A_LAYERS:
            i = layer
            h = _rmsnorm(x, norm_a[i])
            x = x + _short_conv_mixer(h, w_in_a[i], conv_a[i], w_out_a[i])
            if layer == N_A_LAYERS - 1:
                kv = _rmsnorm(x, norm_kv) @ w_kv
                k, v = jnp.split(kv, 2, axis=-1)
                k = k.reshape(bsz, seq, N_HEADS, HEAD_DIM).transpose(0, 2, 1, 3)
                v = v.reshape(bsz, seq, N_HEADS, HEAD_DIM).transpose(0, 2, 1, 3)
        else:
            j = layer - N_A_LAYERS
            h = _rmsnorm(x, norm_b[j])
            q, g = jnp.split(h @ w_in_b[j], 2, axis=-1)
            q = q.reshape(bsz, seq, N_HEADS, HEAD_DIM).transpose(0, 2, 1, 3)
            o = _stick_breaking_attention(q, k, v)
            o = o.transpose(0, 2, 1, 3).reshape(bsz, seq, ATT_WIDTH)
            x = x + (o * jax.nn.silu(g)) @ w_out_b[j]
    return _rmsnorm(x, norm_f)


def setup_inputs(seed=0):
    out = dict(first_inputs(seed))
    for name, value in second_inputs(seed + 1).items():
        if name != "x":
            out[name + "_2"] = value
    return out


def reference(
    x, positions, norm_w, ffn_w_gate, ffn_w_up, ffn_w_down, ssm_w_in, ssm_conv_w, ssm_conv_b,
    ssm_dt_bias, ssm_a_log, ssm_d, ssm_norm_w, ssm_w_out, mla_w_in, mla_q_a_norm, mla_kv_a_norm,
    mla_w_q_b, mla_w_kv_b, mla_q_norm, mla_k_norm, mla_w_out, norm_a_2, w_in_a_2, conv_a_2,
    w_out_a_2, norm_kv_2, w_kv_2, norm_b_2, w_in_b_2, w_out_b_2, norm_f_2,
):
    x = first_block(
        x, positions, norm_w, ffn_w_gate, ffn_w_up, ffn_w_down, ssm_w_in, ssm_conv_w,
        ssm_conv_b, ssm_dt_bias, ssm_a_log, ssm_d, ssm_norm_w, ssm_w_out, mla_w_in,
        mla_q_a_norm, mla_kv_a_norm, mla_w_q_b, mla_w_kv_b, mla_q_norm, mla_k_norm, mla_w_out,
    )
    return second_block(
        x, norm_a_2, w_in_a_2, conv_a_2, w_out_a_2, norm_kv_2, w_kv_2, norm_b_2, w_in_b_2,
        w_out_b_2, norm_f_2,
    )


_drawn_inputs = setup_inputs


def setup_inputs(seed=0):
    import zlib

    import numpy as np

    out = dict(_drawn_inputs(seed))
    spreads = {}
    factors = {'mla_q_a_norm': 7.234,
     'mla_kv_a_norm': 4.603,
     'mla_q_norm': 7.662,
     'mla_k_norm': 7.533,
     'norm_a_2': 3.686,
     'norm_kv_2': 8.0,
     'norm_b_2': 8.0,
     'norm_f_2': 2.858}
    for name, (base, spread) in spreads.items():
        noise = np.random.default_rng([zlib.crc32(name.encode()), seed]).standard_normal(out[name].shape)
        drawn = base * np.exp(spread * noise) if base else spread * noise
        out[name] = __import__('jax').numpy.asarray(drawn.astype(out[name].dtype))
    for name, factor in factors.items():
        out[name] = (out[name] * factor).astype(out[name].dtype)
    return out
```

```python
from contextlib import ExitStack

import numpy as np

import concourse.bass as bass
from concourse import mybir

P = 128
T = 256
TB = T // P
D = 1024
KD = D // P
FF = 2816
KF = FF // P
CW = 256
NC = FF // CW
UNIT = 2048
RING = 4
DI = 2048
G, R, HP = 8, 4, 64
NH = G * R
GW = R * HP
ZXBC = 2 * DI + 2 * G * P
QL, KVL, ROPE, NOPE, VD, MH = 384, 256, 32, 64, 64, 16
QK = NOPE + ROPE
HALF = ROPE // 2
THETA = 10000.0
SH = 8
AW = 512
NEG = -1.0e30
EPS = 1e-6

F32 = mybir.dt.float32
F32R = mybir.dt.float32r
I32 = mybir.dt.int32
ALU = mybir.AluOpType
ACT = mybir.ActivationFunctionType
AX = mybir.AxisListType.X

PHASES = ["ffn0", "mamba", "ffn1", "ffn2", "mla", "ffn3", "conv", "stick"]

SSM_NORM, CQ_NORM, NORM_A, NORM_KV, NORM_B = (2 * P + n for n in (32, 48, 53, 61, 69))


def norm_col(i, j):
    return 8 * (3 * i + j)


def ffn_norm(f):
    return norm_col(f // 2, 2 * (f % 2))


UNITS_OF = {"ffn": [UNIT] * (2 * NC + KF // 2),
            "mamba": [KD * NH] + [UNIT] * 24 + [UNIT] * 8,
            "mla": [UNIT] * 2 + [KD * 160] + [UNIT] * 2 + [3 * 512] * 3 + [UNIT] * 4,
            "conv": [UNIT] * 16 + [UNIT] * 4,
            "stick": [UNIT] * 4 + [UNIT] * 4 + [UNIT] * 2}


def unit_columns():
    return [n for name in PHASES for n in UNITS_OF[name.rstrip("0123")]]


def input_norms(name):
    if name[:3] == "ffn":
        return (ffn_norm(int(name[3])),)
    return {"mamba": (norm_col(0, 1),), "mla": (norm_col(1, 1),), "conv": (NORM_A,),
            "stick": (NORM_KV, NORM_B)}[name]


def unscaled(name):
    return name[:3] == "ffn" or name == "mla"


MAMBA_TURNS = {"acs": 1, "btok": 1, "xs": TB, "seg": 1, "y": 2, "off": 1, "g": TB}
SMALLS = 16 * 7
INV_FREQ = (np.float32(1.0) / np.float32(THETA) ** (np.arange(0, ROPE, 2, dtype=np.float32) / np.float32(ROPE)))
WHOLE = 1.5 * 2.0 ** 23
PI = float(np.float32(3.14159250))
TWO_PI = (6.28125, 1.93500518798828125e-3, 3.0199159819e-7)


def landed_counts():
    counts, slots = [], [0] * RING
    for name in PHASES:
        n = UNITS_OF[name.rstrip("0123")]
        for k in range(len(n)):
            slot = len(counts) % RING
            slots[slot] += 64 if name == "conv" and k < 2 * KD else 32
            counts.append(slots[slot])
    return counts


def conv_tile(s):
    return 16 + 4 * s if s < 4 else 4 * (s - 4)


def mla_rounds():
    return [(0, 0, 8), (0, 8, 8), (1, 0, 4), (1, 4, 4), (1, 8, 4), (1, 12, 4)]


def act_copies(tb, of_q, quad):
    return tb == 0 or not of_q or quad % 2 == 0


def mamba_slots(n):
    found = []
    if n == 8:
        found.append(("acs", 0))
    if n in (4, 6):
        found.append(("btok", (n - 4) // 2))
    if n in (12, 14, 16, 18):
        found.append(("xs", (n - 12) // 2))
    for name, first in (("off", 15), ("y", 14), ("seg", 13)):
        if 0 <= n - first < G:
            found.append((name, n - first))
    if n == 23:
        found += [("g", 0), ("g", 1)]
    if n == 24:
        found += [("g", 2), ("g", 3)]
    return found


class Place:

    def __init__(self):
        self.unit = self.split = self.turn = self.high = 0
        self.pair = 0
        self.gate = self.norm = self.sums = self.scaled = 0
        self.name = self.next = None

    def layers(self):
        for self.name, self.next in zip(PHASES, PHASES[1:] + ["end"]):
            yield self.name


def program(nc, t, out):
    cols_of_unit = unit_columns()
    n_units = len(cols_of_unit)
    landed = landed_counts()
    ctx = ExitStack()
    with ctx:
        def sem(name):
            return ctx.enter_context(nc.semaphore(name))

        def sb(name, shape, dt=F32):
            return ctx.enter_context(nc.sbuf_tensor(name, shape, dt))

        def overlaid(*specs):
            with ExitStack() as inner:
                return [inner.enter_context(nc.sbuf_tensor(*s)) for s in specs]

        raw = sb("raw", [P, RING, UNIT])
        w_hi = sb("w_hi", [P, RING, UNIT], F32R)
        w_lo = sb("w_lo", [P, RING, UNIT], F32R)
        x = sb("x", [P, TB, D])
        xT_hi = sb("xT_hi", [P, KD, T], F32R)
        xT_lo = sb("xT_lo", [P, KD, T], F32R)
        ident = sb("ident", [P, P])
        upto = sb("upto", [P, P])
        from_ = sb("from_", [P, P])
        after_r = sb("after_r", [P, P], F32R)
        ones = sb("ones", [P, P])
        causal = sb("causal", [P, 2, P])
        strict = sb("strict", [P, P])
        cols = sb("cols", [P, 4, P])
        minus_half = sb("minus_half", [P, NH])
        square_sum = sb("square_sum", [P, TB])
        mean_square = sb("mean_square", [P, TB])
        rstd = sb("rstd", [P, TB])
        dt_bias = sb("dt_bias", [P, NH])
        a_log = sb("a_log", [P, NH])
        d_skip = sb("d_skip", [P, NH])
        q_gain = sb("q_gain", [P, QK])
        k_gain = sb("k_gain", [P, QK])
        pos_i = sb("pos_i", [P, TB], I32)
        pos = sb("pos", [P, TB])
        inv_freq = sb("inv_freq", [P, HALF])
        angle = sb("angle", [P, TB, HALF])
        cos = sb("cos", [P, TB, HALF])
        sin = sb("sin", [P, TB, HALF])
        wraps = sb("wraps", [P, TB, HALF])
        hT_hi, hT_lo = overlaid(("hT_hi", [P, KF, T], F32R), ("hT_lo", [P, KF, T], F32R))
        BT, CT, Btok, conv, E, xdt, R_hi, R_lo, cbm, xdtd, state = overlaid(
            ("BT", [P, G, T], F32), ("CT", [P, G, T], F32), ("Btok", [P, G, P], F32),
            ("conv", [P, 4, T], F32), ("E", [P, TB, R * P], F32), ("xdt", [P, 2, TB, GW], F32),
            ("R_hi", [P, TB, R * P], F32R), ("R_lo", [P, TB, R * P], F32R), ("cbm", [P, TB, P], F32),
            ("xdtd", [P, GW], F32), ("state", [P, GW], F32))
        k_tok, qT, kT = overlaid(("k_tok", [P, TB, MH, QK], F32), ("qT", [P, MH, T], F32),
                                 ("kT", [P, MH, T], F32))
        (o_tok,) = overlaid(("o_tok", [P, TB, MH * VD], F32))
        _, q_squares, _, k_squares = overlaid(
            ("_kt", [P, TB, MH, QK], F32), ("q_squares", [P, TB, MH * QK], F32),
            ("_qt", [P, MH * T - TB * MH * QK], F32), ("k_squares", [P, TB, MH * NOPE], F32))
        zr1, _, zmask, zn0, zr0, _, zn1 = overlaid(
            ("zr1", [P, 4, 3 * P], F32), ("_h1", [P, 16 * T - 12 * P], F32), ("zmask", [P, 3 * P], F32),
            ("zn0", [P, 4, 3 * P], F32), ("zr0", [P, 4, 3 * P], F32),
            ("_h2", [P, (KF + 16) * T - 16 * T - 27 * P], F32), ("zn1", [P, 4, 3 * P], F32))
        zn, zr = (zn0, zn1), (zr0, zr1)
        sb("region_h", [P, 2 * KF * T])
        sg, h, junk, xn = overlaid(("sg", [P, TB, CW], F32), ("h", [P, TB, CW], F32),
                                   ("junk", [P, D], F32), ("xn", [P, TB, D], F32))
        (sz, _, ys, xsT, off, dtv, dta, dte, dt, ea, dA, dA_hi, dA_lo, eacs, dend, gss, gms, grs) = overlaid(
            ("sz", [P, TB, 512], F32), ("_junk", [P, D], F32), ("ys", [P, TB, DI], F32),
            ("xsT", [P, 4, T], F32), ("off", [P, GW], F32), ("dtv", [P, TB, NH], F32), ("dta", [P, TB, NH], F32),
            ("dte", [P, TB, NH], F32), ("dt", [P, TB, NH], F32), ("ea", [P, NH], F32),
            ("dA", [P, TB, NH], F32), ("dA_hi", [P, TB, NH], F32R), ("dA_lo", [P, TB, NH], F32),
            ("eacs", [P, NH], F32), ("dend", [P, R], F32), ("gss", [P, TB, G], F32),
            ("gms", [P, TB, G], F32), ("grs", [P, TB, G], F32))
        (kv_tok, q_tok, proj, lss, lms, lrs, kr, rot, qss, qms, qrs, kss, kms, krs) = overlaid(
            ("kv_tok", [P, TB, MH, NOPE + VD], F32), ("q_tok", [P, TB, MH, QK], F32),
            ("proj", [P, TB, QL + KVL + ROPE], F32), ("lss", [P, TB, 3], F32),
            ("lms", [P, TB, 3], F32), ("lrs", [P, TB, 3], F32), ("kr", [P, TB, ROPE], F32),
            ("rot", [P, 4, HALF], F32), ("qss", [P, TB, 2, MH], F32), ("qms", [P, TB, 2, MH], F32),
            ("qrs", [P, TB, 2, MH], F32), ("kss", [P, TB, MH], F32), ("kms", [P, TB, MH], F32),
            ("krs", [P, TB, MH], F32))
        (_, sc, pm, pT, _, top, nbias, psums, pinv) = overlaid(
            ("_kv", [P, TB, MH, NOPE + VD], F32), ("sc", [P, 2, D], F32), ("pm", [P, D], F32),
            ("pT", [P, 8, P], F32), ("_gap", [P, 600], F32), ("top", [P, TB, MH], F32),
            ("nbias", [P, TB, MH], F32), ("psums", [P, TB, MH], F32), ("pinv", [P, TB, MH], F32))
        (_, qrot,) = overlaid(("_kv2", [P, TB, MH, NOPE + VD + QK], F32), ("qrot", [P, 4, MH * HALF], F32))
        (c_sb, g_sb, v_sb, y_sb) = overlaid(("c_sb", [P, T], F32), ("g_sb", [P, T], F32),
                                            ("v_sb", [P, T], F32), ("y_sb", [P, T], F32))
        (s_kT, _, s_v, s_qT, s_g, wt, og) = overlaid(
            ("s_kT", [P, 4, T], F32), ("_xn", [P, D + TB * D], F32), ("s_v", [P, TB, AW], F32),
            ("s_qT", [P, 4, T], F32), ("s_g", [P, 4, T], F32), ("wt", [P, 2, 3 * P], F32),
            ("og", [P, T], F32))
        (f_gain,) = overlaid(("f_gain", [P, D], F32))
        (_, rows, after) = overlaid(("_junk2", [P, 2 * D], F32), ("rows", [P, 4, P], F32), ("after", [P, P], F32))
        sb("region_g", [P, 8960])

        def psum(name, n):
            return ctx.enter_context(nc.psum_tensor(name, [P, n, 512], F32))

        acc = psum("acc", 4)
        tr = psum("tr", 2)
        aux = psum("aux", 2)

        raw_landed = [sem(f"raw_landed{i}") for i in range(RING)]
        hi_ready = sem("hi_ready")
        lo_ready = sem("lo_ready")
        unit_used = sem("unit_used")
        half_done = sem("half_done")
        acc_read = [sem(f"acc_read{i}") for i in range(4)]
        turned = sem("turned")
        turn_hi = sem("turn_hi")
        tr_read = [sem(f"tr_read{i}") for i in range(2)]
        x_landed = [sem(f"x_landed{b}") for b in range(TB)]
        norms_landed = sem("norms_landed")
        rows_landed = sem("rows_landed")
        cols_ready = sem("cols_ready")
        cols_turned = sem("cols_turned")
        small_landed = sem("small_landed")
        consts = sem("consts")
        gated = sem("gated")
        squared = sem("squared")
        rstd_ready = sem("rstd_ready")
        xn_ready = sem("xn_ready")
        pool_chain = sem("pool_chain")
        dve_chain = sem("dve_chain")
        act_chain = sem("act_chain")
        rope_dve = sem("rope_dve")
        rope_act = sem("rope_act")
        tap_ready = sem("tap_ready")
        conv_done = sem("conv_done")
        dt_dve = sem("dt_dve")
        dt_act = sem("dt_act")
        r_ready = sem("r_ready")
        seg_ready = sem("seg_ready")
        exp_done = sem("exp_done")
        m_ready = sem("m_ready")
        xdt_ready = sem("xdt_ready")
        xdtd_ready = sem("xdtd_ready")
        y_done = sem("y_done")
        z_done = sem("z_done")
        z_squared = sem("z_squared")
        z_rstd = sem("z_rstd")
        g_ready = sem("g_ready")
        lat_squared = sem("lat_squared")
        lat_rstd = sem("lat_rstd")
        lat_ready = sem("lat_ready")
        q_squared = sem("q_squared")
        k_squared = sem("k_squared")
        means_ready = sem("means_ready")
        roots_ready = sem("roots_ready")
        k_rstd = sem("k_rstd")
        q_rstd = sem("q_rstd")
        q_scaled = sem("q_scaled")
        score_ready = sem("score_ready")
        nbias_ready = sem("nbias_ready")
        probs_ready = sem("probs_ready")
        o_ready = sem("o_ready")
        o_read = sem("o_read")
        gate_ready = sem("gate_ready")
        y_ready = sem("y_ready")
        yT_hi_ready = sem("yT_hi_ready")
        yT_ready = sem("yT_ready")
        z_ready = sem("z_ready")
        z_read = sem("z_read")
        z_ln = sem("z_ln")
        zl_ready = sem("zl_ready")
        zmask_ready = sem("zmask_ready")
        kr_ready = sem("kr_ready")
        k_scaled = sem("k_scaled")
        f_landed = sem("f_landed")
        after_ready = sem("after_ready")
        w_sum = sem("w_sum")
        w_ready = sem("w_ready")
        heads_done = sem("heads_done")
        og_ready = sem("og_ready")
        oT_hi_ready = sem("oT_hi_ready")
        result_ready = sem("result_ready")
        stored = sem("stored")

        block = ctx.enter_context(nc.Block())

        def bank(p, b):
            return acc[:, 2 * (p % 2) + b, :]

        def acc_done(eng, p, b, more=0):
            if p < 0:
                return
            eng.wait_ge(acc_read[2 * (p % 2) + b], p // 2 + 1 + more)

        def acc_free(inst, p, b):
            inst.then_inc(acc_read[2 * (p % 2) + b], 1)

        def turn_done(eng, k, more=0):
            eng.wait_ge(tr_read[k % 2], k // 2 + 1 + more)

        def turn_free(inst, k):
            inst.then_inc(tr_read[k % 2], 1)

        def col(n):
            return cols[:, n // P, n % P:n % P + 1]

        def z_bank(hd):
            return (tr if hd % 4 < 2 else aux)[:, hd % 2, :]

        inputs_to = ((xT_hi, xT_lo, 0), (hT_hi, hT_lo, 8))

        def matrix(w):
            return w.rearrange("(k p) n -> p k n", p=P)

        def across(v, n):
            return v.rearrange("(a n) -> a n", a=1).to_broadcast([P, n])

        def heads(ap, n):
            return ap.rearrange("p (r l) -> p r l", r=n)

        row_parts = [
            (0, 48, t["norm_w"].rearrange("i j (k p) -> (i j k) p", p=P)),
            (SSM_NORM, 16, t["ssm_norm_w"].rearrange("a (k p) -> (a k) p", p=P)),
            (CQ_NORM, 3, t["mla_q_a_norm"].rearrange("a (k p) -> (a k) p", p=P)),
            (CQ_NORM + 3, 2, t["mla_kv_a_norm"].rearrange("a (k p) -> (a k) p", p=P)),
            (NORM_A, 8, t["norm_a_2"].rearrange("a (k p) -> (a k) p", p=P)),
            (NORM_KV, 8, t["norm_kv_2"].rearrange("(k p) -> k p", p=P)),
            (NORM_B, 8, t["norm_b_2"].rearrange("a (k p) -> (a k) p", p=P)),
            (P, 128, t["ssm_conv_w"].rearrange("a j (k p) -> (a j k) p", p=P)),
            (2 * P, 32, t["ssm_conv_b"].rearrange("a (k p) -> (a k) p", p=P)),
            (3 * P, 24, t["conv_a_2"].rearrange("a j (k p) -> (a j k) p", p=P)),
        ]
        row_tiles = [(0, 48), (1, 128), (2, NORM_B + 8 - 2 * P), (3, 24)]

        @block.sync
        def _(sp):
            c = Place()

            def load_x(b):
                sp.dma_start(x[:, b, :], t["x"][0, b * P:(b + 1) * P, :]).then_inc(x_landed[b], 16)

            def load_rows(part, landed):
                at, count, src = part
                sp.dma_start(rows[at % P:at % P + count, at // P, :], src).then_inc(landed, 16)

            def load(u, pieces, lap=None):
                if lap is not None:
                    sp.wait_ge(lo_ready, lap + (u - RING + 1))
                elif u >= RING:
                    sp.wait_ge(lo_ready, u - RING + 1)
                for dst, src in pieces:
                    sp.dma_start(dst, src).then_inc(raw_landed[u % RING], 16)

            def up_unit(f, u, half, col):
                dst = raw[:, u % RING, :].rearrange("p (k g n) -> p k g n", k=4, g=2)
                return [(dst[:, :, g, :],
                         matrix(t[name][f // 2, f % 2])[:, 4 * half:4 * half + 4, bass.ds(col, CW)])
                        for g, name in enumerate(("ffn_w_gate", "ffn_w_up"))]

            def down_unit(f, u, k0):
                dst = raw[:, u % RING, :].rearrange("p (k n) -> p k n", k=2)
                src = matrix(t["ffn_w_down"][f // 2, f % 2])[:, bass.ds(k0, 2), :]
                return [(dst[:, :, 0:512], src[:, :, 0:512]), (dst[:, :, 512:], src[:, :, 512:])]

            def ffn(f):
                u = c.unit
                if u == 0:
                    for j in range(4):
                        if j == 0:
                            load_x(0)
                            load_rows(row_parts[0], norms_landed)
                        load(j, up_unit(f, j, j % 2, j // 2 * CW))
                        if j == 0:
                            load_x(1)
                        if j == 3:
                            for part in row_parts[1:]:
                                load_rows(part, rows_landed)
                with sp.Fori(0 if u else 1, NC // 2) as i:
                    for j in range(4):
                        load(u + j, up_unit(f, u + j, j % 2, i * (2 * CW) + j // 2 * CW), 4 * i)
                u += 4 * (NC // 2)
                for j in range(2):
                    load(u + j, up_unit(f, u + j, j, (NC - 1) * CW))
                u += 2
                with sp.Fori(0, 2) as i:
                    for j in range(4):
                        load(u + j, down_unit(f, u + j, i * 8 + 2 * j), 4 * i)
                for j in range(8, 11):
                    load(u + j, down_unit(f, u + j, 2 * j))
                c.unit = u + 11

            def whole(w, k_tiles, per, c0, width):
                for k in range(0, k_tiles, per):
                    dst = raw[:, c.unit % RING, 0:per * width].rearrange("p (k n) -> p k n", k=per)
                    src = matrix(w)[:, k:k + per, c0:c0 + width]
                    a = per // 2
                    load(c.unit, [(dst[:, 0:a], src[:, 0:a]), (dst[:, a:], src[:, a:])])
                    c.unit += 1

            def mamba():
                w = t["ssm_w_in"][0]
                whole(w, KD, KD, ZXBC, NH)
                for c0 in (2 * DI, 2 * DI + 512, 2 * DI + 1024, 2 * DI + 1536,
                           DI, DI + 512, DI + 1024, DI + 1536, 0, 512, 1024, 1536):
                    whole(w, KD, 4, c0, 512)
                whole(t["ssm_w_out"][0], DI // P, 2, 0, D)

            def mla():
                whole(t["mla_w_in"][0], KD, 4, 0, 512)
                whole(t["mla_w_in"][0], KD, KD, 512, 160)
                for n in range(2):
                    whole(t["mla_w_kv_b"][0], 2, 2, 1024 * n, 1024)
                for n in range(3):
                    whole(t["mla_w_q_b"][0], 3, 3, 512 * n, 512)
                whole(t["mla_w_out"][0], KD, 2, 0, D)

            def short_conv():
                w = t["w_in_a_2"][0].rearrange("(k p) (g f n) -> p k g f n", p=P, g=4, n=P)
                for f in range(KD):
                    for half in range(2):
                        dst = raw[:, c.unit % RING, :].rearrange("p (k g n) -> p k g n", k=4, g=4)
                        load(c.unit, [(dst[:, :, g, :], w[:, 4 * half:4 * half + 4, g, f, :])
                                      for g in range(4)])
                        c.unit += 1
                whole(t["w_out_a_2"][0], KD, 2, 0, D)

            def stick():
                for w, c0 in ((t["w_kv_2"], AW), (t["w_kv_2"], 0), (t["w_in_b_2"][0], 0), (t["w_in_b_2"][0], AW)):
                    whole(w, KD, 4, c0, AW)
                whole(t["w_out_b_2"][0], AW // P, 2, 0, D)

            run = {"mamba": mamba, "mla": mla, "conv": short_conv, "stick": stick}
            for name in PHASES:
                ffn(int(name[3])) if name[:3] == "ffn" else run[name]()
            assert c.unit == n_units
            sp.wait_ge(heads_done, SH)
            sp.dma_start(f_gain[:], across(t["norm_f_2"], D)).then_inc(f_landed, 16)
            for b in range(TB):
                sp.wait_ge(result_ready, b + 1)
                sp.dma_start(out[0, b * P:(b + 1) * P, :], xn[:, b, :]).then_inc(stored, 16)
            sp.wait_ge(stored, 16 * TB)

        @block.tensor
        def _(pe):
            c = Place()

            def product(o, lh, ll, rh, rl, start, stop, skip=False):
                pe.matmul(o, lh, rh, start=start, stop=False, skip_group_check=skip)
                pe.matmul(o, lh, rl, start=False, stop=False, skip_group_check=skip)
                return pe.matmul(o, ll, rh, start=False, stop=stop, skip_group_check=skip)

            def claim(p, b, more=0):
                acc_done(pe, p - 2, b, more)

            def claim_turn(k, more=0):
                if k >= 2:
                    turn_done(pe, k - 2, more)

            def turn(blocks, k, more=0):
                claim_turn(k, more)
                for at, src in blocks:
                    n = src.free_size()
                    last = pe.transpose(tr[0:n, k % 2, at:at + P], src, ident[:])
                last.then_inc(turned, 1)

            def input_turns(name, tb):
                src = x if unscaled(name) else xn
                for half in range(2):
                    if src is xn:
                        if half == 0:
                            c.scaled += 1
                            pe.wait_ge(xn_ready, c.scaled)
                    elif c.pair:
                        acc_done(pe, c.pair - 2 + tb, half)
                    else:
                        pe.wait_ge(x_landed[tb], 16)
                    turn([(j * P, src[:, tb, (4 * half + j) * P:(4 * half + j + 1) * P])
                          for j in range(4)], c.turn)
                    c.turn += 1

            def first_step(unit_part):
                early = unscaled(c.name)
                k = c.turn - 2 if early else c.turn
                if not early:
                    input_turns(c.name, 0)
                for half in range(2):
                    turn_done(pe, k + half)
                    unit_part(half, 0)
                    if early and half == 0:
                        input_turns(c.name, 1)
                if not early:
                    input_turns(c.name, 1)
                for half in range(2):
                    turn_done(pe, k + 2 + half)
                    unit_part(half, 1)

            def both_blocks():
                for tb in range(TB):
                    input_turns(c.name, tb)
                for tb in range(TB):
                    turn_done(pe, c.turn - 4 + 2 * tb)

            def other_half():
                for tb in range(TB):
                    turn_done(pe, c.turn - 3 + 2 * tb)

            def token_unit(u, p, k0, nk, kt, width, lap=0, tbs=(0, 1), source=(xT_hi, xT_lo), at=0, done=True,
                           stride=None):
                pe.wait_ge(lo_ready, u + 1 + lap)
                stride = stride or width
                for kk in range(nk):
                    for tb in tbs:
                        ts = slice(tb * P, (tb + 1) * P)
                        w = slice(kk * stride + at, kk * stride + at + width)
                        last = product(bank(p, tb)[:, 0:width], source[0][:, k0 + kk, ts], source[1][:, k0 + kk, ts],
                                       w_hi[:, u % RING, w], w_lo[:, u % RING, w],
                                       k0 + kk == 0, k0 + kk == kt - 1)
                if done:
                    last.then_inc(unit_used, 1)

            def feature_unit(u, p, k0, source=(xT_hi, xT_lo), s0=0):
                pe.wait_ge(lo_ready, u + 1)
                for kk in range(4):
                    k = k0 + kk
                    for ft in range(4):
                        w = slice(kk * 512 + ft * P, kk * 512 + ft * P + P)
                        last = product(bank(p, ft // 2)[:, ft % 2 * T:(ft % 2 + 1) * T],
                                       w_hi[:, u % RING, w], w_lo[:, u % RING, w],
                                       source[0][:, s0 + k, :], source[1][:, s0 + k, :],
                                       k == 0 and ft % 2 == 0, k == KD - 1, skip=True)
                last.then_inc(unit_used, 1)

            def sum_units(source, k_tiles, ready, middle=lambda: None):
                u0, p, n_u = c.unit, c.pair, k_tiles // 2
                c.unit += n_u
                c.pair += 2

                def part(n, tb):
                    u = u0 + n
                    ts = slice(tb * P, (tb + 1) * P)
                    if tb == 0:
                        pe.wait_ge(lo_ready, u + 1)
                        ready(n)
                    for kk in range(2):
                        k = 2 * n + kk
                        for nh in range(2):
                            if k == 0:
                                claim(p + tb, nh)
                            w = slice(kk * D + nh * 512, kk * D + nh * 512 + 512)
                            last = product(bank(p + tb, nh), source[0][:, k, ts], source[1][:, k, ts],
                                           w_hi[:, u % RING, w], w_lo[:, u % RING, w],
                                           k == 0, k == k_tiles - 1)
                    if tb:
                        last.then_inc(unit_used, 1)
                    elif n == n_u - 1:
                        last.then_inc(half_done, 1)

                for n in range(n_u - 2):
                    part(n, 0)
                    if n == 0:
                        middle()
                    part(n, 1)
                part(n_u - 2, 0)
                part(n_u - 1, 0)
                part(n_u - 2, 1)
                if c.next != "end" and unscaled(c.next):
                    input_turns(c.next, 0)
                part(n_u - 1, 1)

            def ffn(f):
                u0, p0 = c.unit, c.pair
                claim(p0, 0)
                claim(p0, 1)
                first_step(lambda half, tb: token_unit(u0 + half, p0, 4 * half, 4, KD, 512, tbs=(tb,), done=tb == 1))
                k0 = c.turn

                def h_turn(k, lap=0):
                    for tb in range(TB):
                        acc_done(pe, p0 + (k - k0), tb, lap)
                    turn([(ft * T + tb * P, h[:, tb, ft * P:(ft + 1) * P])
                          for ft in range(2) for tb in range(TB)], k, lap)

                with pe.Fori(0, NC // 2) as i:
                    for j in range(2):
                        u, p = u0 + 2 + 2 * j, p0 + 1 + j
                        for b in range(TB):
                            claim(p, b, i)
                        token_unit(u, p, 0, 4, KD, 512, lap=4 * i)
                        h_turn(k0 + j, i)
                        token_unit(u + 1, p, 4, 4, KD, 512, lap=4 * i)
                c.unit, c.pair, c.turn = u0 + 2 * NC, p0 + NC, k0 + NC
                if f == 0:
                    pe.wait_ge(rows_landed, 16 * (len(row_parts) - 1))
                    for tile in row_tiles[1:]:
                        turn_rows(*tile)
                sum_units((hT_hi, hT_lo), KF, lambda n: turn_done(pe, k0 + n),
                          middle=lambda: h_turn(k0 + NC - 1))

            def mamba():
                pe.wait_ge(consts, 9)
                pe.wait_ge(after_ready, 1)
                for b in range(TB):
                    claim(c.pair, b)
                both_blocks()
                other_half()
                token_unit(c.unit, c.pair, 0, KD, KD, NH)
                c.unit += 1
                c.pair += 1

                def small(n):
                    for name, g in mamba_slots(n):
                        k = c.turn
                        if name == "acs":
                            pe.wait_ge(dt_dve, 2)
                            claim_turn(k)
                            pe.matmul(tr[:, k % 2, 0:NH], upto[:], dA[:, 1, :], start=True, stop=True)\
                                .then_inc(turned, 1)
                            c.turn += 1
                        elif name == "btok":
                            pe.wait_ge(conv_done, g + 1)
                            turn([(j * P, BT[:, 4 * g + j, 0:P]) for j in range(4)], k)
                            c.turn += 1
                        elif name == "xs":
                            pe.wait_ge(conv_done, 4 + g + 1)
                            for tb in range(TB):
                                turn([(j * P, xsT[:, j, tb * P:(tb + 1) * P]) for j in range(4)], c.turn)
                                c.turn += 1
                        elif name == "seg":
                            if g == 0:
                                pe.wait_ge(conv_done, 4)
                            claim_turn(k)
                            for tb in range(TB):
                                ts = slice(tb * P, (tb + 1) * P)
                                last = pe.matmul(tr[:, k % 2, ts], BT[:, g, ts], CT[:, g, ts], start=True, stop=True)
                            last.then_inc(turned, 1)
                            c.turn += 1
                            for tb in range(TB):
                                pe.wait_ge(r_ready, 2 * g + tb + 1)
                                if g:
                                    pe.wait_ge(exp_done, 2 * g + tb - 1)
                                pe.matmul(aux[:, tb, :], after_r[:], R_hi[:, tb, :], start=True, stop=False)
                                pe.matmul(aux[:, tb, :], after_r[:], R_lo[:, tb, :], start=False, stop=True)\
                                    .then_inc(seg_ready, 1)
                        elif name == "y":
                            claim_turn(k)
                            pe.wait_ge(xdt_ready, g + 1)
                            pe.wait_ge(m_ready, 2 * g + 2)
                            for tb in range(TB):
                                for r in range(R):
                                    last = pe.matmul(tr[:, k % 2, tb * GW + r * HP:tb * GW + (r + 1) * HP],
                                                     E[:, tb, r * P:(r + 1) * P],
                                                     xdt[:, g % 2, tb, r * HP:(r + 1) * HP], start=True, stop=True)
                            last.then_inc(turned, 1)
                            claim_turn(k + 1)
                            pe.wait_ge(xdtd_ready, g + 1)
                            pe.matmul(tr[:, (k + 1) % 2, 0:GW], Btok[:, g, :], xdtd[:], start=True, stop=True)\
                                .then_inc(turned, 1)
                            state_turn[g] = k + 1
                            c.turn += 2
                        elif name == "off":
                            claim_turn(k)
                            turn_done(pe, state_turn[g])
                            pe.matmul(tr[:, k % 2, 0:GW], CT[:, g, P:T], state[:], start=True, stop=True)\
                                .then_inc(turned, 1)
                            c.turn += 1
                        elif name == "g":
                            pe.wait_ge(g_ready, g + 1)
                            for tb in range(TB):
                                turn([(j * P, ys[:, tb, g * 512 + j * P:g * 512 + (j + 1) * P])
                                      for j in range(4)], c.turn)
                                c.turn += 1

                state_turn = {}
                for s in range(12):
                    for b in range(TB):
                        claim(c.pair, b)
                    for half in range(2):
                        if s < 8:
                            feature_unit(c.unit, c.pair, 4 * half)
                        else:
                            token_unit(c.unit, c.pair, 4 * half, 4, KD, 512)
                        c.unit += 1
                        small(2 * s + half)
                    c.pair += 1
                kg = c.turn - 4

                def gated_ready(n):
                    if n == 1:
                        small(24)
                    for tb in range(TB):
                        turn_done(pe, kg + 2 * (n // 2) + tb)

                sum_units((hT_hi, hT_lo), DI // P, gated_ready)

            def mla():
                for b in range(TB):
                    claim(c.pair, b)
                first_step(lambda half, tb: token_unit(c.unit + half, c.pair, 4 * half, 4, KD, 512, tbs=(tb,),
                                                       done=tb == 1))
                c.unit += 2
                c.pair += 1
                for b in range(TB):
                    claim(c.pair, b)
                token_unit(c.unit, c.pair, 0, KD, KD, 160)
                c.unit += 1
                c.pair += 1
                for tb in range(TB):
                    pe.wait_ge(lat_ready, 2 * tb + 2)
                    turn([(j * P, proj[:, tb, j * P:(j + 1) * P]) for j in range(4)], c.turn)
                    turn([(0, proj[:, tb, 4 * P:5 * P])], c.turn + 1)
                    c.turn += 2
                for q in range(4):
                    turn_done(pe, c.turn - 4 + q)
                kv_latent = (xT_hi[:, 3:5, :], xT_lo[:, 3:5, :])
                for n in range(2):
                    for nh in range(2):
                        for b in range(TB):
                            claim(c.pair, b)
                        token_unit(c.unit, c.pair, 0, 2, 2, 512, source=kv_latent, at=512 * nh,
                                   stride=1024, done=nh == 1)
                        c.pair += 1
                    c.unit += 1
                for n in range(3):
                    for b in range(TB):
                        claim(c.pair, b)
                    token_unit(c.unit, c.pair, 0, 3, 3, 512)
                    c.unit += 1
                    c.pair += 1
                for src, scaled in ((k_tok, k_scaled), (q_tok, q_scaled)):
                    for tb in range(TB):
                        pe.wait_ge(scaled, tb + 1)
                        for quad in range(4):
                            turn([(j * P, src[:, tb, 4 * quad + j, :]) for j in range(4)], c.turn)
                            c.turn += 1
                rounds = mla_rounds()
                k_last = c.turn

                def scores(r):
                    tb, h0, nh = rounds[r]
                    if r == 0:
                        turn_done(pe, k_last - 1)
                        turn_done(pe, k_last - 2)
                    per = nh // 2
                    for b in range(2):
                        claim(c.pair + r, b)
                        for j in range(per):
                            hd = h0 + b * per + j
                            w = P * (tb + 1)
                            last = pe.matmul(bank(c.pair + r, b)[:, j * w:(j + 1) * w], qT[0:QK, hd, tb * P:(tb + 1) * P],
                                             kT[0:QK, hd, 0:w], start=True, stop=True)
                        last.then_inc(score_ready, 1)

                def values(r):
                    tb, h0, nh = rounds[r]
                    pe.wait_ge(probs_ready, r + 1)
                    for b in range(2):
                        turn([(j * P, pm[:, (4 * b + j) * P:(4 * b + j + 1) * P]) for j in range(4)], c.turn)
                        c.turn += 1
                    turn_done(pe, c.turn - 2)
                    turn_done(pe, c.turn - 1)
                    if r >= 2:
                        pe.wait_ge(o_read, r - 1)
                    for j in range(nh):
                        for kb in range(tb + 1):
                            last = pe.matmul(aux[:, r % 2, j * VD:(j + 1) * VD], pT[:, j * (tb + 1) + kb, :],
                                             kv_tok[:, kb, h0 + j, NOPE:], start=kb == 0, stop=kb == tb)
                    last.then_inc(o_ready, 1)

                scores(0)
                for r in range(len(rounds)):
                    if r + 1 < len(rounds):
                        scores(r + 1)
                    values(r)
                c.pair += len(rounds)
                for tb in range(TB):
                    pe.wait_ge(o_read, (2, 6)[tb])
                    for half in range(2):
                        turn([(j * P, o_tok[:, tb, (4 * half + j) * P:(4 * half + j + 1) * P])
                              for j in range(4)], c.turn)
                        c.turn += 1
                for q in range(4):
                    turn_done(pe, c.turn - 4 + q)
                sum_units((xT_hi, xT_lo), KD, lambda n: None)

            def short_conv():
                for f in range(KD):
                    for b in range(TB):
                        claim(c.pair, b)
                    if f == 0:
                        both_blocks()
                    for half in range(2):
                        if f == 0 and half:
                            other_half()
                        feature_unit(c.unit + half, c.pair, 4 * half)
                    c.unit += 2
                    c.pair += 1
                sum_units((hT_hi, hT_lo), KD, lambda n: pe.wait_ge(yT_ready, 2 * n + 2))

            def stick():
                def scores(hd, o, extra):
                    ps = slice(64 * (hd % 2), 64 * (hd % 2) + 64)
                    ks, qs = s_kT[ps, hd // 2, :], s_qT[ps, hd // 2, :]
                    if not extra:
                        pe.matmul(o[:, 0:T], ks[:, 0:P], qs, start=True, stop=True)
                        return pe.matmul(o[:, T:3 * P], ks[:, P:T], qs[:, P:T], start=True, stop=True)
                    zl = zr[hd // 4][:, hd % 4, :]
                    zl0, zl1 = zl[:, 0:T], zl[:, T:3 * P]
                    pe.matmul(o[:, 0:T], ks[:, 0:P], qs, start=True, stop=False, skip_group_check=True)
                    pe.matmul(o[:, 0:T], from_[:], zl0, start=False, stop=False, skip_group_check=True)
                    pe.matmul(o[:, P:T], ones[:], zl1, start=False, stop=False, skip_group_check=True)
                    pe.matmul(o[:, 0:P], ident[:], strict[:], start=False, stop=True, skip_group_check=True)
                    o1 = o[:, T:3 * P]
                    pe.matmul(o1, ks[:, P:T], qs[:, P:T], start=False, stop=False, skip_group_check=True)
                    pe.matmul(o1, from_[:], zl1, start=False, stop=False, skip_group_check=True)
                    return pe.matmul(o1, ident[:], strict[:], start=False, stop=True, skip_group_check=True)

                k0 = c.turn + 4

                def logits(hd):
                    if hd == 0:
                        for p in (c.pair - 1, c.pair - 2, c.pair - 3):
                            for b in range(TB):
                                acc_done(pe, p, b)
                    if hd % 4 < 2:
                        claim_turn(k0 + hd // 4 * 2 + hd % 2)
                    elif hd >= 4:
                        pe.wait_ge(z_read, hd - 5)
                    scores(hd, z_bank(hd), False).then_inc(z_ready, 1)

                for n in range(4):
                    for b in range(TB):
                        claim(c.pair, b)
                    if n == 0:
                        first_step(lambda half, tb: token_unit(c.unit + half, c.pair, 4 * half, 4, KD, 512,
                                                               tbs=(tb,), done=tb == 1))
                    for half in range(2):
                        if n == 1:
                            feature_unit(c.unit + half, c.pair, 4 * half)
                        elif n > 1:
                            feature_unit(c.unit + half, c.pair, 4 * half, (hT_hi, hT_lo), 8)
                        if n == 3:
                            for hd in range(4 * half, 4 * half + 4):
                                logits(hd)
                    c.unit += 2
                    c.pair += 1

                c.turn += 4
                p0 = c.pair

                def weights(hd):
                    pe.wait_ge(zl_ready, hd // 4 + 1)
                    if hd >= 2:
                        pe.wait_ge(w_ready, hd - 1)
                    else:
                        pe.wait_ge(z_read, hd + 3)
                    scores(hd, aux[:, hd % 2, :], True).then_inc(w_sum, 1)

                def values(hd):
                    pe.wait_ge(w_ready, hd + 1)
                    p, b = p0 + hd // 4, hd // 2 % 2
                    if hd % 2 == 0:
                        claim(p, b)
                    o = bank(p, b)[64 * (hd % 2):64 * (hd % 2) + 64, 0:T]
                    vs = slice(64 * hd, 64 * hd + 64)
                    w = wt[:, hd % 2, :]
                    pe.matmul(o, s_v[:, 0, vs], w[:, 0:T], start=True, stop=False, skip_group_check=True)
                    pe.matmul(o[:, P:T], s_v[:, 1, vs], w[:, T:3 * P], start=False, stop=True, skip_group_check=True)\
                        .then_inc(heads_done, 1)

                weights(0)
                weights(1)
                for hd in range(SH):
                    values(hd)
                    if hd + 2 < SH:
                        weights(hd + 2)
                c.pair += SH // 4
                sum_units((xT_hi, xT_lo), AW // P, lambda n: (acc_done(pe, p0 + n, 0), acc_done(pe, p0 + n, 1)))

            def turn_rows(n, count):
                pe.transpose(aux[:, n == 0, n % 4 * P:n % 4 * P + count], rows[0:count, n, :],
                             ident[0:count, 0:count]).then_inc(cols_turned, 1)

            pe.wait_ge(consts, 1)
            pe.wait_ge(norms_landed, 16)
            turn_rows(*row_tiles[0])
            run = {"mamba": mamba, "mla": mla, "conv": short_conv, "stick": stick}
            if unscaled(PHASES[0]):
                input_turns(PHASES[0], 0)
            for name in c.layers():
                ffn(int(name[3])) if name[:3] == "ffn" else run[name]()

        @block.scalar
        def _(act):
            c = Place()
            linked = [0]

            def link(inst):
                linked[0] += 1
                inst.then_inc(act_chain, 1)
                act.wait_ge(act_chain, linked[0])

            def split(u, lap=None):
                n = cols_of_unit[u]
                if lap is None:
                    act.wait_ge(raw_landed[u % RING], landed[u])
                    if u >= RING:
                        act.wait_ge(unit_used, u - RING + 1)
                else:
                    act.wait_ge(raw_landed[u % RING], lap * (32 // RING) + landed[u])
                    act.wait_ge(unit_used, lap + (u - RING + 1))
                act.activation(w_hi[:, u % RING, 0:n], raw[:, u % RING, 0:n], ACT.Copy).then_inc(hi_ready, 1)

            def split_to(u):
                while c.split < min(u, n_units):
                    split(c.split)
                    c.split += 1

            def high(dst, at, k, scale, last):
                inst = act.activation(dst, tr[:, k % 2, at:at + P], ACT.Copy, scale=scale)
                if last:
                    inst.then_inc(turn_hi, 1)

            def input_high(tb):
                for half in range(2):
                    act.wait_ge(turned, c.turn + 1)
                    for norm, (dst, _, s0) in zip(input_norms(c.name), inputs_to):
                        for j in range(4):
                            high(dst[:, s0 + 4 * half + j, tb * P:(tb + 1) * P], j * P, c.turn,
                                 col(norm + 4 * half + j), j == 3)
                    c.turn += 1

            def squares_of_x(tb):
                if c.pair:
                    for b in range(2):
                        acc_done(act, c.pair - 2 + tb, b)
                else:
                    act.wait_ge(x_landed[tb], 16)
                if tb:
                    act.wait_ge(squared, c.norm)
                act.activation(junk[:], x[:, tb, :], ACT.Square,
                               accum_out=square_sum[:, tb:tb + 1]).then_inc(squared, 1)
                c.norm += 1

            def layer_input():
                for tb in range(TB):
                    if not unscaled(c.name):
                        squares_of_x(tb)
                        act.wait_ge(rstd_ready, c.norm)
                        act.activation(xn[:, tb, :], x[:, tb, :], ACT.Copy, scale=rstd[:, tb:tb + 1])\
                            .then_inc(xn_ready, 1)
                    input_high(tb)
                    if c.unit == 0:
                        split_to(2 * tb + 2)
                    if tb == 0 and c.name == "mamba":
                        split_to(c.unit + 3)
                if unscaled(c.name):
                    squares_of_x(0)
                    squares_of_x(1)

            def sums(k_tiles):
                c.unit += k_tiles // 2
                c.pair += 2
                split_to(c.unit + 2)

            def ffn(f):
                u0, p0 = c.unit, c.pair
                layer_input()
                k0 = c.turn
                split_to(u0 + 4)
                act.wait_ge(rstd_ready, c.norm)

                def gate(n, lap=0):
                    act.wait_ge(unit_used, lap * 4 + (u0 + 2 * n + 2))
                    for tb in range(TB):
                        act.activation(sg[:, tb, :], bank(p0 + n, tb)[:, 0:CW], ACT.Silu,
                                       scale=rstd[:, tb:tb + 1]).then_inc(gated, 1)

                def hidden_high(n, at, lap=0):
                    k = k0 + n
                    act.wait_ge(turned, lap * 2 + (k + 1))
                    act.activation(hT_hi[:, bass.ds(at, 2), :].rearrange("p f t -> p (f t)"), tr[:, k % 2, :],
                                   ACT.Copy).then_inc(turn_hi, 1)

                with act.Fori(0, NC // 2) as i:
                    for j in range(2):
                        gate(j, i)
                        for v in range(2):
                            split(u0 + 4 + 2 * j + v, 4 * i)
                        hidden_high(j, i * 4 + 2 * j, i)
                c.split = u0 + 2 * NC + 2
                gate(NC - 1)
                split_to(u0 + 2 * NC + 4)
                hidden_high(NC - 1, 2 * (NC - 1))
                c.unit, c.pair, c.turn = u0 + 2 * NC, p0 + NC, k0 + NC
                if f == 0:
                    rotation()
                    act.wait_ge(cols_ready, len(row_tiles))
                sums(KF)

            def mamba():
                layer_input()
                c.unit += 1
                c.pair += 1
                p0, u0 = c.pair, c.unit
                split_to(u0 + 3)

                def time_steps():
                    act.wait_ge(small_landed, SMALLS)
                    act.activation(ea[:], a_log[:], ACT.Exp).then_inc(dt_act, 1)
                    act.wait_ge(dt_dve, 1)
                    link(act.activation(dte[:], dta[:], ACT.Exp, scale=-1.0))
                    act.activation(dta[:], dte[:], ACT.Ln, bias=1.0).then_inc(dt_act, 1)
                    act.wait_ge(dt_dve, 2)
                    act.activation(dA_hi[:], dA[:], ACT.Copy).then_inc(dt_act, 1)

                def small(n):
                    for name, g in mamba_slots(n):
                        k = c.turn
                        c.turn += MAMBA_TURNS[name]
                        if name == "acs":
                            act.wait_ge(turned, k + 1)
                            turn_free(act.activation(eacs[:], tr[:, k % 2, 0:NH], ACT.Exp), k)
                        elif name == "btok":
                            act.wait_ge(turned, k + 1)
                            turn_free(act.activation(Btok[:, 4 * g:4 * g + 4, :].rearrange("p g n -> p (g n)"),
                                                     tr[:, k % 2, :], ACT.Copy), k)
                        elif name == "xs":
                            for tb in range(TB):
                                act.wait_ge(turned, k + tb + 1)
                                turn_free(act.activation(ys[:, tb, 512 * g:512 * (g + 1)], tr[:, (k + tb) % 2, :],
                                                         ACT.Copy), k + tb)
                        elif name == "seg":
                            for tb in range(TB):
                                act.wait_ge(seg_ready, 2 * g + tb + 1)
                                if tb == 0:
                                    act.activation(dend[:], aux[:, 0, P - 1::P], ACT.Exp)
                                act.activation(E[:, tb, :], aux[:, tb, :], ACT.Exp).then_inc(exp_done, 1)
                        elif name == "y":
                            act.wait_ge(turned, k + 2)
                            inst = act.activation(state[:], tr[:, (k + 1) % 2, 0:GW], ACT.Copy)
                            turn_free(inst, k + 1)
                        elif name == "g":
                            for tb in range(TB):
                                act.wait_ge(turned, k + tb + 1)
                                for j in range(4):
                                    high(hT_hi[:, 4 * g + j, tb * P:(tb + 1) * P], j * P, k + tb,
                                         col(SSM_NORM + 4 * g + j), j == 3)

                def first_tap(s):
                    act.wait_ge(unit_used, u0 + 2 * s + 2)
                    p = p0 + s
                    if s < 8:
                        if s:
                            act.wait_ge(conv_done, s)
                        for ft in range(4):
                            tile = conv_tile(s) + ft
                            act.activation(conv[:, ft, :], bank(p, ft // 2)[:, ft % 2 * T:(ft % 2 + 1) * T],
                                           ACT.Identity, scale=col(P + 3 * 32 + tile),
                                           bias=col(2 * P + tile)).then_inc(tap_ready, 1)
                    else:
                        for tb in range(TB):
                            if s > 8:
                                act.wait_ge(z_done, 2 * (s - 9) + tb + 1)
                            acc_free(act.activation(sz[:, tb, :], bank(p, tb), ACT.Silu), p, tb)

                def finish_step(s):
                    if s < 8:
                        dst = BT if s < 2 else CT if s < 4 else xsT
                        for b in range(2):
                            acc_done(act, p0 + s, b)
                            t0 = (4 * (s % 2) if s < 4 else 0) + 2 * b
                            inst = act.activation(dst[:, t0:t0 + 2, :], conv[:, 2 * b:2 * b + 2, :], ACT.Silu)
                        inst.then_inc(conv_done, 1)
                    else:
                        j = s - 8
                        if j:
                            act.wait_ge(z_squared, j)
                        for tb in range(TB):
                            act.wait_ge(z_done, 2 * j + tb + 1)
                            for g in (2 * j, 2 * j + 1):
                                at = (2 * tb + g - 2 * j) * GW
                                inst = act.activation(junk[:, at:at + GW], ys[:, tb, g * GW:(g + 1) * GW], ACT.Square,
                                                      accum_out=gss[:, tb, g:g + 1])
                        inst.then_inc(z_squared, 1)

                for s in range(12):
                    if s:
                        first_tap(s - 1)
                    split_to(u0 + 2 * s + 3)
                    small(2 * s)
                    split_to(u0 + 2 * s + 4)
                    if s:
                        finish_step(s - 1)
                    else:
                        time_steps()
                    small(2 * s + 1)
                first_tap(11)
                finish_step(11)
                small(24)
                c.unit, c.pair = u0 + 24, p0 + 12
                sums(DI // P)

            def mla():
                layer_input()
                split_to(c.unit + 4)
                act.wait_ge(rstd_ready, c.norm)
                for first, width, n_u in ((0, 512, 2), (512, 160, 1)):
                    c.unit += n_u
                    split_to(c.unit + 2)
                    act.wait_ge(unit_used, c.unit)
                    for tb in range(TB):
                        acc_free(act.activation(proj[:, tb, first:first + width], bank(c.pair, tb)[:, 0:width],
                                                ACT.Copy, scale=rstd[:, tb:tb + 1]), c.pair, tb)
                    c.pair += 1
                lat_parts = ((0, QL), (QL, KVL), (QL + KVL, ROPE))
                act.wait_ge(acc_read[2 * ((c.pair - 1) % 2) + 1], (c.pair - 1) // 2 + 1)
                act.wait_ge(acc_read[2 * ((c.pair - 2) % 2) + 1], (c.pair - 2) // 2 + 1)
                for tb in range(TB):
                    for n, (at, w) in enumerate(lat_parts):
                        to = tb * (QL + KVL + ROPE) + at
                        inst = act.activation(q_squares[:, 0, to:to + w], proj[:, tb, at:at + w], ACT.Square,
                                              accum_out=lss[:, tb, n:n + 1])
                inst.then_inc(lat_squared, 1)
                act.wait_ge(lat_rstd, 1)
                for tb in range(TB):
                    for n, (at, w) in enumerate(lat_parts[:2]):
                        act.activation(proj[:, tb, at:at + w], proj[:, tb, at:at + w], ACT.Copy,
                                       scale=lrs[:, tb, n:n + 1]).then_inc(lat_ready, 1)
                for tb in range(TB):
                    for j in range(5):
                        if j % 4 == 0:
                            act.wait_ge(turned, c.turn + 1)
                        high(xT_hi[:, j, tb * P:(tb + 1) * P], j % 4 * P, c.turn, col(CQ_NORM + j), j >= 3)
                        c.turn += j >= 3
                q_flat = q_tok[:].rearrange("p b h d -> p b (h d)")
                kv_flat = kv_tok[:].rearrange("p b h d -> p b (h d)")

                def root(n):
                    act.wait_ge(means_ready, n + 1)
                    act.activation((krs, qrs)[n][:], (kms, qms)[n][:], ACT.Sqrt).then_inc(roots_ready, 1)

                for n in range(4):
                    if n % 2 == 0:
                        c.unit += 1
                        split_to(c.unit + 2)
                        act.wait_ge(unit_used, c.unit)
                    acc_free(act.activation(kv_flat[:, 0, 512 * n:512 * (n + 1)], bank(c.pair, 0), ACT.Copy),
                             c.pair, 0)
                    c.pair += 1
                for n in range(3):
                    c.unit += 1
                    split_to(c.unit + 2)
                    if n < TB:
                        for m in range(4):
                            acc_done(act, c.pair - n - 4 + m, n)
                        act.activation(k_squares[:, n, :].rearrange("p (h d) -> p h d", h=MH),
                                       kv_tok[:, n, :, 0:NOPE], ACT.Square).then_inc(k_squared, 1)
                    else:
                        root(0)
                    act.wait_ge(unit_used, c.unit)
                    acc_free(act.activation(q_flat[:, 0, 512 * n:512 * (n + 1)], bank(c.pair, 0), ACT.Copy),
                             c.pair, 0)
                    c.pair += 1
                for tb in range(TB):
                    for n in range(3):
                        acc_done(act, c.pair - 3 + n, tb)
                    act.activation(q_squares[:, tb, :], q_flat[:, tb, :], ACT.Square).then_inc(q_squared, 1)
                root(1)
                for dst in (kT, qT):
                    for tb in range(TB):
                        for quad in range(4):
                            if act_copies(tb, dst is qT, quad):
                                act.wait_ge(turned, c.turn + 1)
                                turn_free(act.activation(
                                    dst[0:QK, 4 * quad:4 * quad + 4, tb * P:(tb + 1) * P],
                                    tr[0:QK, c.turn % 2, :].rearrange("p (h l) -> p h l", h=4), ACT.Copy), c.turn)
                            c.turn += 1
                rounds = mla_rounds()
                for r, (tb, h0, nh) in enumerate(rounds):
                    w = P * (tb + 1)
                    act.wait_ge(nbias_ready, r + 1)
                    act.wait_ge(turned, c.turn)
                    for j in range(nh):
                        hd = h0 + j
                        inst = act.activation(pm[:, j * w:(j + 1) * w], sc[:, r % 2, j * w:(j + 1) * w], ACT.Exp,
                                              bias=nbias[:, tb, hd:hd + 1], scale=QK ** -0.5,
                                              accum_out=psums[:, tb, hd:hd + 1])
                    inst.then_inc(probs_ready, 1)
                    act.wait_ge(turned, c.turn + 1)
                    if r:
                        act.wait_ge(o_ready, r)
                    turn_free(act.activation(pT[:, 0:4, :].rearrange("p h l -> p (h l)"), tr[:, c.turn % 2, :],
                                             ACT.Copy), c.turn)
                    c.turn += 2
                c.pair += len(rounds)
                for tb in range(TB):
                    for half in range(2):
                        act.wait_ge(turned, c.turn + 1)
                        act.activation(xT_hi[:, 4 * half:4 * half + 4, tb * P:(tb + 1) * P],
                                       tr[:, c.turn % 2, :].rearrange("p (h l) -> p h l", h=4), ACT.Copy)\
                            .then_inc(turn_hi, 1)
                        c.turn += 1
                split_to(c.unit + 4)
                sums(KD)

            def short_conv():
                layer_input()
                for f in range(KD + 1):
                    if f:
                        p = c.pair + f - 1
                        act.wait_ge(unit_used, c.unit + 2 * f)
                        if f > 1:
                            act.wait_ge(y_ready, f - 1)
                        act.activation(c_sb[:], bank(p, 0)[:, T:2 * T], ACT.Copy)
                        act.activation(g_sb[:], bank(p, 1)[:, T:2 * T], ACT.Silu).then_inc(gate_ready, 1)
                    split_to(c.unit + 2 * f + 4)
                    if f:
                        act.wait_ge(y_ready, f)
                        act.activation(hT_hi[:, f - 1, :], y_sb[:], ACT.Copy).then_inc(yT_hi_ready, 1)
                c.unit += 2 * KD
                c.pair += KD
                sums(KD)

            def stick():
                layer_input()

                def soft(four):
                    act.wait_ge(z_read, 2 * four + 2)
                    for r in (1, 2):
                        turn_done(act, c.turn + 2 * four + 2 - r)
                    link(act.activation(zn[four][:], zn[four][:], ACT.Exp))
                    act.activation(zn[four][:], zn[four][:], ACT.Ln, bias=1.0).then_inc(z_ln, 1)

                for n in range(4):
                    split_to(c.unit + 4)
                    c.unit += 2
                    if n == 3:
                        soft(0)
                    else:
                        act.wait_ge(unit_used, c.unit)
                    p = c.pair
                    if n < 3:
                        dst = (s_v[:, 0, :], s_kT[:, 0:2, :].rearrange("p f t -> p (f t)"),
                               s_qT[:, 0:2, :].rearrange("p f t -> p (f t)"))[n]
                        acc_free(act.activation(dst, bank(p, 0), ACT.Copy, scale=0.125 if n == 2 else 1.0), p, 0)
                    else:
                        for b in range(2):
                            if b == 0:
                                act.wait_ge(unit_used, c.unit)
                            acc_free(act.activation(s_g[:, 2 * b:2 * b + 2, :].rearrange("p f t -> p (f t)"),
                                                    bank(p, b), ACT.Silu), p, b)
                    c.pair += 1

                def weights(hd):
                    act.wait_ge(w_sum, hd + 1)
                    if hd >= 2:
                        act.wait_ge(heads_done, hd - 1)
                    act.activation(wt[:, hd % 2, :], aux[:, hd % 2, 0:3 * P], ACT.Exp).then_inc(w_ready, 1)

                soft(1)
                for hd in range(SH):
                    weights(hd)
                    if hd % 2:
                        j = hd // 2
                        act.wait_ge(og_ready, j + 1)
                        act.activation(xT_hi[:, j, :], og[:], ACT.Copy).then_inc(oT_hi_ready, 1)
                c.pair += SH // 4
                sums(AW // P)
                squares_of_x(0)
                squares_of_x(1)

            def rotation():
                act.wait_ge(rope_dve, 1)
                act.activation(sin[:], sin[:], ACT.Sin)
                act.activation(cos[:], cos[:], ACT.Sin).then_inc(rope_act, 1)
                act.wait_ge(consts, 4)
                act.activation(after_r[:], after[:], ACT.Copy).then_inc(after_ready, 1)

            split_to(1)
            act.wait_ge(cols_ready, 1)
            run = {"mamba": mamba, "mla": mla, "conv": short_conv, "stick": stick}
            for name in c.layers():
                ffn(int(name[3])) if name[:3] == "ffn" else run[name]()

        @block.vector
        def _(dve):
            c = Place()
            linked = [0]

            def note(inst):
                linked[0] += 1
                inst.then_inc(dve_chain, 1)
                return linked[0]

            def link(inst):
                dve.wait_ge(dve_chain, note(inst))

            def split(u, lap=0):
                n = cols_of_unit[u]
                dve.wait_ge(hi_ready, u + 1 + lap)
                dve.tensor_tensor(w_lo[:, u % RING, 0:n], raw[:, u % RING, 0:n],
                                  w_hi[:, u % RING, 0:n].bitcast(F32), ALU.subtract).then_inc(lo_ready, 1)

            def split_to(u):
                while c.split < min(u, n_units):
                    split(c.split)
                    c.split += 1

            def low(dst, hi, at, k, scale, last):
                inst = dve.scalar_tensor_tensor(dst, tr[:, k % 2, at:at + P], scale, hi.bitcast(F32),
                                                ALU.mult, ALU.subtract)
                if last:
                    turn_free(inst, k)

            def input_low(name, tb):
                norms = input_norms(name)
                for half in range(2):
                    c.high += len(norms)
                    dve.wait_ge(turn_hi, c.high)
                    for n, (norm, (hi, lo, s0)) in enumerate(zip(norms, inputs_to)):
                        for j in range(4):
                            at = (slice(None), s0 + 4 * half + j, slice(tb * P, (tb + 1) * P))
                            low(lo[at], hi[at], j * P, c.turn, col(norm + 4 * half + j),
                                j == 3 and n == len(norms) - 1)
                    c.turn += 1

            def layer_input():
                if not unscaled(c.name):
                    input_low(c.name, 0)
                if c.unit == 0:
                    split_to(2)
                if c.name == "mamba":
                    split_to(c.unit + 3)
                input_low(c.name, 1)
                c.norm += 1

            def result(tb):
                dve.wait_ge(rstd_ready, 2 * c.norm + tb + 1)
                if tb == 0:
                    dve.wait_ge(f_landed, 16)
                for b in range(2):
                    acc_done(dve, c.pair + tb, b)
                dve.scalar_tensor_tensor(xn[:, tb, :], x[:, tb, :], rstd[:, tb:tb + 1], f_gain[:],
                                         ALU.mult, ALU.mult).then_inc(result_ready, 1)

            def sums(k_tiles, scale):
                c.unit += k_tiles // 2
                split_to(c.unit + 2)
                c.sums += 1
                if c.sums == 1:
                    for landed_x in x_landed:
                        dve.wait_ge(landed_x, 16)
                for tb in range(TB):
                    if tb:
                        dve.wait_ge(unit_used, c.unit)
                    else:
                        dve.wait_ge(half_done, c.sums)
                    for nh in range(2):
                        xs = x[:, tb, 512 * nh:512 * (nh + 1)]
                        acc_free(dve.scalar_tensor_tensor(xs, bank(c.pair + tb, nh), scale, xs, ALU.mult, ALU.add),
                                 c.pair + tb, nh)
                    if c.next == "end":
                        result(tb)
                    elif tb == 0 and unscaled(c.next):
                        input_low(c.next, 0)
                c.pair += 2

            def ffn(f):
                u0, p0 = c.unit, c.pair
                layer_input()
                k0, h0, g0 = c.turn, c.high, c.gate
                split_to(u0 + 4)
                dve.wait_ge(rstd_ready, 2 * c.norm)

                def hidden(n, lap=0):
                    for tb in range(TB):
                        dve.wait_ge(gated, lap * 4 + (g0 + 2 * n + tb + 1))
                        acc_free(dve.scalar_tensor_tensor(h[:, tb, :], bank(p0 + n, tb)[:, CW:2 * CW],
                                                          rstd[:, tb:tb + 1], sg[:, tb, :], ALU.mult, ALU.mult),
                                 p0 + n, tb)

                def hidden_low(n, at, lap=0):
                    k = k0 + n
                    dve.wait_ge(turn_hi, lap * 2 + (h0 + n + 1))
                    turn_free(dve.tensor_tensor(
                        hT_lo[:, bass.ds(at, 2), :].rearrange("p f t -> p (f t)"), tr[:, k % 2, :],
                        hT_hi[:, bass.ds(at, 2), :].rearrange("p f t -> p (f t)").bitcast(F32), ALU.subtract), k)

                with dve.Fori(0, NC // 2) as i:
                    for j in range(2):
                        hidden(j, i)
                        for v in range(2):
                            split(u0 + 4 + 2 * j + v, 4 * i)
                        hidden_low(j, i * 4 + 2 * j, i)
                c.split = u0 + 2 * NC + 2
                hidden(NC - 1)
                split_to(u0 + 2 * NC + 4)
                hidden_low(NC - 1, 2 * (NC - 1))
                c.unit, c.pair, c.turn = u0 + 2 * NC, p0 + NC, k0 + NC
                c.high, c.gate = h0 + NC, g0 + 2 * NC
                if f == 0:
                    for tile in row_tiles[1:]:
                        copy_columns(*tile)
                    rotation()
                    dve.wait_ge(cols_ready, len(row_tiles))
                sums(KF, 0.5)

            def mamba():
                layer_input()
                c.unit += 1
                c.pair += 1
                p0, u0 = c.pair, c.unit
                split_to(u0 + 3)

                def time_steps():
                    dve.wait_ge(unit_used, u0)
                    dve.wait_ge(small_landed, SMALLS)
                    for tb in range(TB):
                        acc_free(dve.tensor_tensor(dtv[:, tb, :], bank(p0 - 1, tb)[:, 0:NH], dt_bias[:], ALU.add),
                                 p0 - 1, tb)
                    for tb in range(TB):
                        acc_done(dve, p0 - 1, tb)
                    dve.scalar_tensor_tensor(dta[:], dtv[:], -1.0, dtv[:], ALU.mult, ALU.max).then_inc(dt_dve, 1)
                    dve.wait_ge(dt_act, 2)
                    link(dve.scalar_tensor_tensor(dt[:], dtv[:], 0.0, dta[:], ALU.max, ALU.add))
                    for tb in range(TB):
                        inst = dve.scalar_tensor_tensor(dA[:, tb, :], dt[:, tb, :], -1.0, ea[:], ALU.mult, ALU.mult)
                    inst.then_inc(dt_dve, 1)
                    dve.wait_ge(dt_act, 3)
                    dve.tensor_tensor(dA_lo[:], dA[:], dA_hi[:].bitcast(F32), ALU.subtract).then_inc(dt_dve, 1)

                def small(n):
                    for name, g in mamba_slots(n):
                        k = c.turn
                        c.turn += MAMBA_TURNS[name]
                        if name == "seg":
                            dve.wait_ge(turned, k + 1)
                            inst = dve.tensor_tensor(cbm[:], tr[:, k % 2, 0:T].rearrange("p (b l) -> p b l", b=TB),
                                                     upto[:].unsqueeze(1).to_broadcast([P, TB, P]), ALU.mult)
                            turn_free(inst, k)
                            turn_done(dve, k)
                            for tb in range(TB):
                                dve.wait_ge(exp_done, 2 * g + tb + 1)
                                e = heads(E[:, tb, :], R)
                                dve.tensor_tensor(e, e, cbm[:, tb, :].unsqueeze(1).to_broadcast([P, R, P]), ALU.mult)\
                                    .then_inc(m_ready, 1)
                        elif name == "y":
                            dve.wait_ge(turned, k + 1)
                            v = ys[:, :, g * GW:(g + 1) * GW]
                            turn_free(dve.tensor_tensor(v, tr[:, k % 2, :].rearrange("p (b c) -> p b c", b=TB), v,
                                                        ALU.add), k)
                        elif name == "off":
                            dve.wait_ge(turned, k + 1)
                            if g == 0:
                                turn_done(dve, acs_turn[0])
                            inst = dve.tensor_tensor(heads(off[:], R), heads(tr[:, k % 2, 0:GW], R),
                                                     eacs[:, R * g:R * g + R].unsqueeze(2).to_broadcast([P, R, HP]),
                                                     ALU.mult)
                            turn_free(inst, k)
                            turn_done(dve, k)
                            v = ys[:, 1, g * GW:(g + 1) * GW]
                            dve.tensor_tensor(v, v, off[:], ALU.add).then_inc(y_done, 1)
                        elif name == "acs":
                            acs_turn.append(k)
                        elif name == "g":
                            for tb in range(TB):
                                c.high += 1
                                dve.wait_ge(turn_hi, c.high)
                                for j in range(4):
                                    at = (slice(None), 4 * g + j, slice(tb * P, (tb + 1) * P))
                                    low(hT_lo[at], hT_hi[at], j * P, k + tb, col(SSM_NORM + 4 * g + j), j == 3)

                def taps(s):
                    p = p0 + s
                    if s < 8:
                        for b in range(2):
                            last = {}
                            for tap in (2, 1, 0):
                                for ft in (2 * b, 2 * b + 1):
                                    if tap == 2:
                                        dve.wait_ge(tap_ready, 4 * s + 2 * b + 2)
                                    else:
                                        dve.wait_ge(dve_chain, last[ft])
                                    d = 3 - tap
                                    v = conv[:, ft, d:]
                                    inst = dve.scalar_tensor_tensor(
                                        v, bank(p, b)[:, ft % 2 * T:(ft % 2 + 1) * T - d],
                                        col(P + tap * 32 + conv_tile(s) + ft), v, ALU.mult, ALU.add)
                                    if tap:
                                        last[ft] = note(inst)
                            acc_free(inst, p, b)
                    else:
                        j = s - 8
                        dve.wait_ge(y_done, 2 * j + 2)
                        for tb in range(TB):
                            acc_done(dve, p, tb)
                            v = ys[:, tb, 512 * j:512 * (j + 1)]
                            dve.tensor_tensor(v, v, sz[:, tb, :], ALU.mult).then_inc(z_done, 1)

                def finish_step(s):
                    if s >= 8:
                        j = s - 8
                        dve.wait_ge(z_rstd, j + 1)
                        for tb in range(TB):
                            for g in (2 * j, 2 * j + 1):
                                v = ys[:, tb, g * GW:(g + 1) * GW]
                                inst = dve.tensor_scalar(v, v, grs[:, tb, g:g + 1], None, ALU.mult)
                        inst.then_inc(g_ready, 1)

                acs_turn = []
                for s in range(12):
                    if s:
                        taps(s - 1)
                    split_to(u0 + 2 * s + 3)
                    small(2 * s)
                    split_to(u0 + 2 * s + 4)
                    if s:
                        finish_step(s - 1)
                    else:
                        time_steps()
                    small(2 * s + 1)
                taps(11)
                finish_step(11)
                small(24)
                c.unit, c.pair = u0 + 24, p0 + 12
                sums(DI // P, 1.0)

            def mla():
                layer_input()
                split_to(c.unit + 4)
                c.unit += 2
                split_to(c.unit + 2)
                c.unit += 1
                split_to(c.unit + 2)
                c.pair += 2
                dve.wait_ge(lat_rstd, 1)
                dve.wait_ge(small_landed, SMALLS)
                for tb in range(TB):
                    inst = dve.scalar_tensor_tensor(kr[:, tb, :], proj[:, tb, QL + KVL:], lrs[:, tb, 2:3],
                                                    k_gain[:, NOPE:], ALU.mult, ALU.mult)
                inst.then_inc(kr_ready, 1)
                for tb in range(TB):
                    for j in range(5):
                        if j % 4 == 0:
                            c.high += 1
                            dve.wait_ge(turn_hi, c.high)
                        at = (slice(None), j, slice(tb * P, (tb + 1) * P))
                        low(xT_lo[at], xT_hi[at], j % 4 * P, c.turn, col(CQ_NORM + j), j >= 3)
                        c.turn += j >= 3
                q_flat = q_tok[:].rearrange("p b h d -> p b (h d)")
                kv_flat = kv_tok[:].rearrange("p b h d -> p b (h d)")

                def root(n):
                    rs, ms, ss = ((krs, kms, kss), (qrs, qms, qss))[n]
                    dve.wait_ge(roots_ready, n + 1)
                    link(dve.reciprocal(rs[:], rs[:]))
                    link(dve.tensor_tensor(ss[:], rs[:], rs[:], ALU.mult))
                    link(dve.tensor_tensor(ss[:], ss[:], ms[:], ALU.mult))
                    link(dve.tensor_scalar(ss[:], ss[:], -0.5, 1.5, ALU.mult, ALU.add))
                    dve.tensor_tensor(rs[:], rs[:], ss[:], ALU.mult).then_inc((k_rstd, q_rstd)[n], 1)

                for n in range(4):
                    if n % 2 == 0:
                        c.unit += 1
                        split_to(c.unit + 2)
                        dve.wait_ge(unit_used, c.unit)
                    acc_free(dve.tensor_copy(kv_flat[:, 1, 512 * n:512 * (n + 1)], bank(c.pair, 1)), c.pair, 1)
                    c.pair += 1
                for n in range(3):
                    c.unit += 1
                    split_to(c.unit + 2)
                    if n == 1:
                        for tb in range(TB):
                            dve.wait_ge(k_squared, tb + 1)
                            link(dve.tensor_reduce(kss[:, tb, :], k_squares[:, tb, :].rearrange("p (h d) -> p h d", h=MH),
                                                   AX, ALU.add))
                        dve.tensor_scalar(kms[:], kss[:], 1.0 / NOPE, EPS, ALU.mult, ALU.add).then_inc(means_ready, 1)
                    if n == 2:
                        root(0)
                    dve.wait_ge(unit_used, c.unit)
                    acc_free(dve.tensor_copy(q_flat[:, 1, 512 * n:512 * (n + 1)], bank(c.pair, 1)), c.pair, 1)
                    c.pair += 1
                for tb in range(TB):
                    dve.wait_ge(q_squared, tb + 1)
                    sq = q_squares[:, tb, :].rearrange("p (h d) -> p h d", h=MH)
                    dve.tensor_reduce(qss[:, tb, 0, :], sq[:, :, 0:NOPE], AX, ALU.add)
                    link(dve.tensor_reduce(qss[:, tb, 1, :], sq[:, :, NOPE:], AX, ALU.add))
                for n, w in enumerate((NOPE, ROPE)):
                    inst = dve.tensor_scalar(qms[:, :, n, :], qss[:, :, n, :], 1.0 / w, EPS, ALU.mult, ALU.add)
                inst.then_inc(means_ready, 1)
                root(1)
                dve.wait_ge(q_rstd, 1)
                dve.wait_ge(rope_act, 1)
                for tb in range(TB):
                    q = q_tok[:, tb, :, :]
                    for n, (a, b) in enumerate(((0, NOPE), (NOPE, QK))):
                        link(dve.tensor_tensor(q[:, :, a:b], q[:, :, a:b],
                                               qrs[:, tb, n, :].unsqueeze(2).to_broadcast([P, MH, b - a]), ALU.mult))
                    link(dve.tensor_tensor(q, q, q_gain[:].unsqueeze(1).to_broadcast([P, MH, QK]), ALU.mult))
                    x1, x2 = q[:, :, NOPE:NOPE + HALF], q[:, :, NOPE + HALF:]
                    cs = cos[:, tb, :].unsqueeze(1).to_broadcast([P, MH, HALF])
                    sn = sin[:, tb, :].unsqueeze(1).to_broadcast([P, MH, HALF])
                    rt = [qrot[:, n, :].rearrange("p (h d) -> p h d", h=MH) for n in range(4)]
                    for n, (v, w) in enumerate(((x1, cs), (x2, sn), (x2, cs), (x1, sn))):
                        inst = dve.tensor_tensor(rt[n], v, w, ALU.mult)
                    link(inst)
                    dve.tensor_tensor(x1, rt[0], rt[1], ALU.subtract)
                    dve.tensor_tensor(x2, rt[2], rt[3], ALU.add).then_inc(q_scaled, 1)
                    dve.wait_ge(q_scaled, tb + 1)
                for dst in (kT, qT):
                    for tb in range(TB):
                        for quad in range(4):
                            if not act_copies(tb, dst is qT, quad):
                                dve.wait_ge(turned, c.turn + 1)
                                turn_free(dve.tensor_copy(
                                    dst[0:QK, 4 * quad:4 * quad + 4, tb * P:(tb + 1) * P],
                                    tr[0:QK, c.turn % 2, :].rearrange("p (h l) -> p h l", h=4)), c.turn)
                            c.turn += 1
                rounds = mla_rounds()

                def masked(r):
                    tb, h0, nh = rounds[r]
                    w, per = P * (tb + 1), nh // 2
                    if r == 0:
                        dve.wait_ge(turned, c.turn)
                    if r >= 2:
                        dve.wait_ge(probs_ready, r - 1)
                    mask = causal[:, 1 - tb:, :].rearrange("p b l -> p (b l)")
                    for b in range(2):
                        dve.wait_ge(score_ready, 2 * r + b + 1)
                        acc_free(dve.tensor_tensor(heads(sc[:, r % 2, 512 * b:512 * (b + 1)], per),
                                                   heads(bank(c.pair + r, b), per),
                                                   mask.unsqueeze(1).to_broadcast([P, per, w]), ALU.add),
                                 c.pair + r, b)
                    for b in range(2):
                        acc_done(dve, c.pair + r, b)
                    hs = slice(h0, h0 + nh)
                    link(dve.tensor_reduce(top[:, tb, hs], heads(sc[:, r % 2, :], nh), AX, ALU.max))
                    dve.tensor_scalar(nbias[:, tb, hs], top[:, tb, hs], -(QK ** -0.5), None, ALU.mult)\
                        .then_inc(nbias_ready, 1)

                masked(0)
                for r, (tb, h0, nh) in enumerate(rounds):
                    if r + 1 < len(rounds):
                        masked(r + 1)
                    hs = slice(h0, h0 + nh)
                    dve.wait_ge(turned, c.turn + 2)
                    if r:
                        dve.wait_ge(o_ready, r)
                    turn_free(dve.tensor_copy(pT[:, 4:8, :].rearrange("p h l -> p (h l)"),
                                              tr[:, (c.turn + 1) % 2, :]), c.turn + 1)
                    c.turn += 2
                    dve.wait_ge(probs_ready, r + 1)
                    link(dve.reciprocal(pinv[:, tb, hs], psums[:, tb, hs]))
                    dve.wait_ge(o_ready, r + 1)
                    dve.tensor_tensor(heads(o_tok[:, tb, h0 * VD:(h0 + nh) * VD], nh), heads(aux[:, r % 2, 0:nh * VD], nh),
                                      pinv[:, tb, hs].unsqueeze(2).to_broadcast([P, nh, VD]), ALU.mult)\
                        .then_inc(o_read, 1)
                c.pair += len(rounds)
                for tb in range(TB):
                    for half in range(2):
                        c.high += 1
                        dve.wait_ge(turn_hi, c.high)
                        at = (slice(None), slice(4 * half, 4 * half + 4), slice(tb * P, (tb + 1) * P))
                        turn_free(dve.tensor_tensor(xT_lo[at], tr[:, c.turn % 2, :].rearrange("p (h l) -> p h l", h=4),
                                                    xT_hi[at].bitcast(F32), ALU.subtract), c.turn)
                        c.turn += 1
                split_to(c.unit + 4)
                sums(KD, 1.0)

            def short_conv():
                layer_input()
                for f in range(KD + 1):
                    if f:
                        p = c.pair + f - 1
                        dve.wait_ge(gate_ready, f)
                        acc_free(dve.tensor_tensor(v_sb[:], bank(p, 1)[:, 0:T], c_sb[:], ALU.mult), p, 1)
                        acc_done(dve, p, 1)
                        w = [col(3 * P + tap * KD + f - 1) for tap in range(3)]
                        link(dve.tensor_scalar(y_sb[:], v_sb[:], w[2], None, ALU.mult))
                        for d in (1, 2):
                            link(dve.scalar_tensor_tensor(y_sb[:, d:], v_sb[:, 0:T - d], w[2 - d], y_sb[:, d:],
                                                          ALU.mult, ALU.add))
                        acc_free(dve.tensor_tensor(y_sb[:], bank(p, 0)[:, 0:T], y_sb[:], ALU.mult), p, 0)
                        acc_done(dve, p, 0)
                        dve.tensor_tensor(y_sb[:], y_sb[:], g_sb[:], ALU.mult).then_inc(y_ready, 1)
                    split_to(c.unit + 2 * f + 4)
                    if f:
                        dve.wait_ge(yT_hi_ready, f)
                        dve.tensor_tensor(hT_lo[:, f - 1, :], y_sb[:], hT_hi[:, f - 1, :].bitcast(F32), ALU.subtract)\
                            .then_inc(yT_ready, 1)
                c.unit += 2 * KD
                c.pair += KD
                sums(KD, 1.0)

            def stick():
                layer_input()
                for n in range(4):
                    split_to(c.unit + 4)
                    c.unit += 2
                    if n < 3:
                        dve.wait_ge(unit_used, c.unit)
                        dst = (s_v[:, 1, :], s_kT[:, 2:4, :].rearrange("p f t -> p (f t)"),
                               s_qT[:, 2:4, :].rearrange("p f t -> p (f t)"))[n]
                        acc_free(dve.tensor_scalar(dst, bank(c.pair, 1), 0.125 if n == 2 else 1.0, None, ALU.mult),
                                 c.pair, 1)
                    c.pair += 1

                def read_logits(four):
                    for r in range(4):
                        dve.wait_ge(z_ready, 4 * four + r + 1)
                        z = z_bank(r)[:, 0:3 * P]
                        link(dve.tensor_scalar(zr[four][:, r, :], z, 0.0, None, ALU.max))
                        inst = dve.scalar_tensor_tensor(zn[four][:, r, :], zr[four][:, r, :], -2.0, z,
                                                        ALU.mult, ALU.add)
                        if r < 2:
                            turn_free(inst, c.turn)
                            c.turn += 1
                        else:
                            inst.then_inc(z_read, 1)

                def soft(four):
                    v = zr[four][:]
                    dve.wait_ge(z_ln, four + 1)
                    dve.wait_ge(z_read, 2 * four + 2)
                    turn_done(dve, c.turn - 1)
                    turn_done(dve, c.turn - 2)
                    link(dve.tensor_tensor(v, v, zn[four][:], ALU.add))
                    dve.wait_ge(zmask_ready, 2)
                    dve.tensor_tensor(v, v, zmask[:].unsqueeze(1).to_broadcast([P, 4, 3 * P]), ALU.mult)\
                        .then_inc(zl_ready, 1)

                for four in range(2):
                    read_logits(four)
                    soft(four)
                for hd in range(SH):
                    if hd % 2:
                        j = hd // 2
                        p, b = c.pair + j // 2, j % 2
                        dve.wait_ge(heads_done, hd + 1)
                        if j:
                            acc_done(dve, c.pair + (j - 1) // 2, (j - 1) % 2)
                        inst = dve.tensor_tensor(og[:], bank(p, b)[:, 0:T], s_g[:, j, :], ALU.mult)
                        inst.then_inc(og_ready, 1)
                        dve.wait_ge(oT_hi_ready, j + 1)
                        acc_free(dve.tensor_tensor(xT_lo[:, j, :], og[:], xT_hi[:, j, :].bitcast(F32), ALU.subtract),
                                 p, b)
                c.pair += SH // 4
                sums(AW // P, 1.0)

            def copy_columns(n, count):
                dve.wait_ge(cols_turned, n + 1)
                dve.tensor_copy(cols[:, n, 0:count], aux[:, n == 0, n % 4 * P:n % 4 * P + count]).then_inc(cols_ready, 1)

            def rotation():
                dve.wait_ge(small_landed, SMALLS)
                dve.wait_ge(consts, 9)
                link(dve.tensor_copy(pos[:], pos_i[:]))
                for tb in range(TB):
                    link(dve.tensor_scalar(angle[:, tb, :], inv_freq[:], pos[:, tb:tb + 1], None, ALU.mult))
                link(dve.tensor_scalar(wraps[:], angle[:], 1.0 / (2.0 * np.pi), WHOLE, ALU.mult, ALU.add))
                link(dve.tensor_scalar(wraps[:], wraps[:], -WHOLE, None, ALU.add))
                for part in TWO_PI:
                    link(dve.scalar_tensor_tensor(angle[:], wraps[:], -part, angle[:], ALU.mult, ALU.add))
                link(dve.tensor_scalar(angle[:], angle[:], PI, -PI, ALU.min, ALU.max))
                link(dve.tensor_scalar(cos[:], angle[:], PI / 2, None, ALU.add))
                link(dve.tensor_scalar(wraps[:], cos[:], PI, -2 * PI, ALU.is_gt, ALU.mult))
                link(dve.tensor_tensor(cos[:], cos[:], wraps[:], ALU.add))
                link(dve.tensor_scalar(cos[:], cos[:], PI, -PI, ALU.min, ALU.max))
                dve.tensor_copy(sin[:], angle[:]).then_inc(rope_dve, 1)

            copy_columns(*row_tiles[0])
            dve.wait_ge(cols_ready, 1)
            split_to(1)
            run = {"mamba": mamba, "mla": mla, "conv": short_conv, "stick": stick}
            if unscaled(PHASES[0]):
                input_low(PHASES[0], 0)
            for name in c.layers():
                ffn(int(name[3])) if name[:3] == "ffn" else run[name]()

        @block.gpsimd
        def _(pool):
            c = Place()
            linked = [0]

            def link(inst):
                linked[0] += 1
                inst.then_inc(pool_chain, 1)
                pool.wait_ge(pool_chain, linked[0])

            def select(m, base, cm, step, op, keep, fill):
                link(pool.memset(m, keep))
                pool.affine_select(out=m, in_=m, compare_op=op, fill=fill, base=base,
                                   pattern=[[step, P]], channel_multiplier=cm).then_inc(consts, 1)

            select(ident[:], 0, 1, -1, ALU.not_equal, 0.0, 1.0)
            select(upto[:], 0, -1, 1, ALU.is_ge, 1.0, 0.0)
            select(from_[:], 0, 1, -1, ALU.is_ge, 1.0, 0.0)
            select(after[:], 0, 1, -1, ALU.is_gt, 1.0, 0.0)
            pool.memset(ones[:], 1.0).then_inc(consts, 1)
            select(strict[:], 0, -1, 1, ALU.is_gt, 0.0, NEG)
            link(pool.memset(causal[:, 0, :], 0.0))
            select(causal[:, 1, :], 0, 1, -1, ALU.is_ge, 0.0, NEG)
            pool.memset(minus_half[:], -0.5).then_inc(consts, 1)
            for n in range(HALF):
                inst = pool.memset(inv_freq[:, n:n + 1], float(INV_FREQ[n]))
            inst.then_inc(consts, 1)
            for dst, src, n in ((dt_bias, t["ssm_dt_bias"][0], NH), (a_log, t["ssm_a_log"][0], NH),
                                (d_skip, t["ssm_d"][0], NH), (q_gain, t["mla_q_norm"][0], QK),
                                (k_gain, t["mla_k_norm"][0], QK)):
                pool.dma_start(dst[:], across(src, n)).then_inc(small_landed, 16)
            with nc.allow_non_contiguous_dma(reason="256 positions"):
                for tb in range(TB):
                    pool.dma_start(pos_i[:, tb:tb + 1], t["positions"][0, tb * P:(tb + 1) * P].rearrange("(p a) -> p a", a=1))\
                        .then_inc(small_landed, 16)

            def norm():
                for tb in range(TB):
                    c.norm += 1
                    pool.wait_ge(squared, c.norm)
                    b = slice(tb, tb + 1)
                    link(pool.tensor_scalar(mean_square[:, b], square_sum[:, b], 1.0 / D, EPS, ALU.mult, ALU.add))
                    pool.tensor_tensor(rstd[:, b], mean_square[:, b], minus_half[:, b], ALU.pow)\
                        .then_inc(rstd_ready, 1)

            def mamba():
                norm()
                c.turn += 4

                def small(n):
                    for name, g in mamba_slots(n):
                        k = c.turn
                        c.turn += MAMBA_TURNS[name]
                        if name == "xs":
                            xs_turn[g] = k
                        elif name == "seg":
                            if g == 0:
                                pool.wait_ge(dt_dve, 3)
                            for tb in range(TB):
                                if g:
                                    pool.wait_ge(seg_ready, 2 * g + tb - 1)
                                for dst, v in ((R_hi, dA_hi[:].bitcast(F32)), (R_lo, dA_lo[:])):
                                    inst = pool.tensor_tensor(
                                        heads(dst[:, tb, :], R), upto[:].unsqueeze(1).to_broadcast([P, R, P]),
                                        v[:, tb, R * g:R * g + R].unsqueeze(2).to_broadcast([P, R, P]), ALU.mult)
                                inst.then_inc(r_ready, 1)
                        elif name == "y":
                            for tb in range(TB):
                                turn_done(pool, xs_turn[g // 2] + tb)
                            for tb in range(TB):
                                v = heads(ys[:, tb, g * GW:(g + 1) * GW], R)
                                link(pool.tensor_tensor(heads(xdt[:, g % 2, tb, :], R), v,
                                                        dt[:, tb, R * g:R * g + R].unsqueeze(2)
                                                        .to_broadcast([P, R, HP]), ALU.mult))
                                inst = pool.tensor_tensor(v, v, d_skip[:, R * g:R * g + R].unsqueeze(2)
                                                          .to_broadcast([P, R, HP]), ALU.mult)
                            inst.then_inc(xdt_ready, 1)
                            pool.wait_ge(exp_done, 2 * g + 1)
                            pool.tensor_tensor(heads(xdtd[:], R), heads(xdt[:, g % 2, 0, :], R),
                                               dend[:].unsqueeze(2).to_broadcast([P, R, HP]), ALU.mult)\
                                .then_inc(xdtd_ready, 1)

                def gated_norm(j):
                    pool.wait_ge(z_squared, j + 1)
                    gs = (slice(None), slice(None), slice(2 * j, 2 * j + 2))
                    link(pool.tensor_scalar(gms[gs], gss[gs], 1.0 / GW, EPS, ALU.mult, ALU.add))
                    pool.tensor_tensor(grs[gs], gms[gs], minus_half[:, 0:4].rearrange("p (a b) -> p a b", a=2),
                                       ALU.pow).then_inc(z_rstd, 1)

                xs_turn = {}
                for n in range(24):
                    small(n)
                    if n in (18, 20, 22):
                        gated_norm((n - 18) // 2)
                gated_norm(3)

            def mla():
                norm()
                pool.wait_ge(lat_squared, 1)
                for n, w in enumerate((QL, KVL, ROPE)):
                    link(pool.tensor_scalar(lms[:, :, n], lss[:, :, n], 1.0 / w, EPS, ALU.mult, ALU.add))
                pool.tensor_tensor(lrs[:], lms[:], minus_half[:, 0:6].rearrange("p (a b) -> p a b", a=2),
                                   ALU.pow).then_inc(lat_rstd, 1)
                pool.wait_ge(kr_ready, 1)
                pool.wait_ge(rope_act, 1)
                for tb in range(TB):
                    x1, x2 = kr[:, tb, 0:HALF], kr[:, tb, HALF:]
                    cs, sn = cos[:, tb, :], sin[:, tb, :]
                    for n, (v, w) in enumerate(((x1, cs), (x2, sn), (x2, cs), (x1, sn))):
                        link(pool.tensor_tensor(rot[:, n, :], v, w, ALU.mult))
                    link(pool.tensor_tensor(x1, rot[:, 0, :], rot[:, 1, :], ALU.subtract))
                    link(pool.tensor_tensor(x2, rot[:, 2, :], rot[:, 3, :], ALU.add))
                pool.wait_ge(k_rstd, 1)
                for tb in range(TB):
                    kn = k_tok[:, tb, :, 0:NOPE]
                    link(pool.tensor_tensor(kn, kv_tok[:, tb, :, 0:NOPE],
                                            krs[:, tb, :].unsqueeze(2).to_broadcast([P, MH, NOPE]), ALU.mult))
                    link(pool.tensor_tensor(kn, kn, k_gain[:, 0:NOPE].unsqueeze(1).to_broadcast([P, MH, NOPE]),
                                            ALU.mult))
                    pool.tensor_copy(k_tok[:, tb, :, NOPE:], kr[:, tb, :].unsqueeze(1).to_broadcast([P, MH, ROPE]))\
                        .then_inc(k_scaled, 1)

            def short_conv():
                norm()

            def stick():
                norm()
                link(pool.memset(zmask[:], -1.0))
                for at in (0, T):
                    pool.affine_select(out=zmask[:, at:at + P], in_=zmask[:, at:at + P], compare_op=ALU.is_gt,
                                       fill=0.0, base=0, pattern=[[1, P]], channel_multiplier=-1)\
                        .then_inc(zmask_ready, 1)
                norm()

            run = {"mamba": mamba, "mla": mla, "conv": short_conv, "stick": stick}
            for name in c.layers():
                if name[:3] == "ffn":
                    norm()
                    c.turn += 4 + NC
                else:
                    run[name]()


INS = ["x", "positions", "norm_w", "ffn_w_gate", "ffn_w_up", "ffn_w_down", "ssm_w_in", "ssm_conv_w",
       "ssm_conv_b", "ssm_dt_bias", "ssm_a_log", "ssm_d", "ssm_norm_w", "ssm_w_out", "mla_w_in",
       "mla_q_a_norm", "mla_kv_a_norm", "mla_w_q_b", "mla_w_kv_b", "mla_q_norm", "mla_k_norm", "mla_w_out",
       "norm_a_2", "w_in_a_2", "conv_a_2", "w_out_a_2", "norm_kv_2", "w_kv_2", "norm_b_2", "w_in_b_2",
       "w_out_b_2", "norm_f_2"]


def kernel(**inputs):
    import concourse.bacc as bacc
    from concourse.bass_utils import run_bass_kernel_spmd

    nc = bacc.Bacc("TRN2", target_bir_lowering=False, num_devices=1)
    arrays, tensors = {}, {}
    for name in INS:
        a = np.ascontiguousarray(inputs[name])
        arrays[f"in_{name}"] = a
        tensors[name] = nc.dram_tensor(f"in_{name}", a.shape, mybir.dt.from_np(a.dtype), kind="ExternalInput").ap()
    out = nc.dram_tensor("out_0", (1, T, D), F32, kind="ExternalOutput").ap()
    program(nc, tensors, out)
    r = run_bass_kernel_spmd(nc, [arrays], core_ids=[0])
    return r.results[0]["out_0"]
```
